# Optimizing a Trainium2 kernel written in Bass

```python
import jax, jax.numpy as jnp
from jax import lax
import numpy as np

D_MODEL = 2048
BATCH = 1
SEQ = 256
DEPTH = 2

GRID_W = 64
CTX_LEN = 256

D_MIX = D_MODEL
D_CONV = D_MIX // 4
D_LRU = D_MIX // 4
HEAD_DIM = 128
N_Q_HEADS = (D_MIX // 2) // HEAD_DIM
N_KV_HEADS = 2
GQA_GROUP = N_Q_HEADS // N_KV_HEADS
D_ATTN = N_Q_HEADS * HEAD_DIM
D_KV = N_KV_HEADS * HEAD_DIM

CONV_WIDTH = 31
LRU_CONV_WIDTH = 4
LRU_BLOCKS = 8
LRU_BLOCK = D_LRU // LRU_BLOCKS
LRU_C = 8.0
WINDOW = 128
Q_BLOCK = 128
ROPE_BASE = 10000.0
EPS = 1e-6

OFF_LRU_X = 0
OFF_K = OFF_LRU_X + D_LRU
OFF_V = OFF_K + D_KV
OFF_MEM_END = OFF_V + D_KV
OFF_CONV_GLU = OFF_MEM_END
OFF_CONV_GATE = OFF_CONV_GLU + 2 * D_CONV
OFF_LRU_GATE = OFF_CONV_GATE + D_CONV
OFF_Q = OFF_LRU_GATE + D_LRU
OFF_ATTN_GATE = OFF_Q + D_ATTN
D_IN = OFF_ATTN_GATE + D_ATTN

kernel_name = "hybrid_conv_rglru_swa_prefix_dit"

def rmsnorm(x, g):
    xf = x.astype(jnp.float32)
    y = xf * lax.rsqrt(jnp.mean(xf * xf, axis=-1, keepdims=True) + EPS)
    return (y * g.astype(jnp.float32)).astype(x.dtype)

def layernorm(x, g, b):
    xf = x.astype(jnp.float32)
    mu = jnp.mean(xf, axis=-1, keepdims=True)
    var = jnp.mean(jnp.square(xf - mu), axis=-1, keepdims=True)
    y = (xf - mu) * lax.rsqrt(var + EPS)
    return (y * g.astype(jnp.float32) + b.astype(jnp.float32)).astype(x.dtype)

def modulate(x, norm_g, ada):
    shift, scale, gate = jnp.split(ada, 3, axis=-1)
    return rmsnorm(x, norm_g) * (1 + scale) + shift, gate

def depthwise_conv(x, w, b, pad):
    y = lax.conv_general_dilated(x, w[:, None, :].astype(x.dtype), window_strides=(1,), padding=[pad],
                                 dimension_numbers=("NWC", "WIO", "NWC"), feature_group_count=x.shape[-1])
    return y + b

def axial_rope_tables(L):
    rows = L // GRID_W
    row = jnp.repeat(jnp.arange(rows, dtype=jnp.float32), GRID_W)
    col = jnp.tile(jnp.arange(GRID_W, dtype=jnp.float32), rows)
    half = HEAD_DIM // 2
    inv = ROPE_BASE ** (-jnp.arange(0, half, 2, dtype=jnp.float32) / half)
    ang_r = row[:, None] * inv[None, :]
    ang_c = col[:, None] * inv[None, :]
    ang = jnp.concatenate([ang_r, ang_r, ang_c, ang_c], axis=-1)
    return jnp.cos(ang), jnp.sin(ang)

def _rotate_half(t):
    t1, t2 = jnp.split(t, 2, axis=-1)
    return jnp.concatenate([-t2, t1], axis=-1)

def apply_axial_rope(x, cos, sin):
    xf = x.astype(jnp.float32)
    xr, xc = jnp.split(xf, 2, axis=-1)
    xrot = jnp.concatenate([_rotate_half(xr), _rotate_half(xc)], axis=-1)
    return (xf * cos[:, None, :] + xrot * sin[:, None, :]).astype(x.dtype)

def sink_softmax(logits, sink_b):
    full = jnp.concatenate([logits, jnp.broadcast_to(sink_b, logits.shape[:-1] + (1,))], axis=-1)
    return jax.nn.softmax(full, axis=-1)[..., :-1]

def conv_branch(u_glu, u_gate, dw_w, dw_b, ln_g, ln_b, pw_w, pw_b):
    a, b = jnp.split(u_glu, 2, axis=-1)
    y = a * jax.nn.sigmoid(b)
    pad = (CONV_WIDTH - 1) // 2
    y = depthwise_conv(y, dw_w, dw_b, (pad, pad))
    y = jax.nn.silu(layernorm(y, ln_g, ln_b))
    y = y @ pw_w + pw_b
    return y * jax.nn.silu(u_gate)

def rglru_scan(x, h0, conv_w, conv_b, w_r, b_r, w_i, b_i, lam):
    xc = depthwise_conv(x, conv_w, conv_b, (LRU_CONV_WIDTH - 1, 0))
    xb = xc.reshape(xc.shape[:-1] + (LRU_BLOCKS, LRU_BLOCK))
    r = jax.nn.sigmoid(jnp.einsum("blhi,hij->blhj", xb, w_r).reshape(xc.shape) + b_r)
    i = jax.nn.sigmoid(jnp.einsum("blhi,hij->blhj", xb, w_i).reshape(xc.shape) + b_i)
    log_a = -LRU_C * r.astype(jnp.float32) * jax.nn.softplus(-lam.astype(jnp.float32))
    a = jnp.exp(log_a)
    bx = jnp.sqrt(-jnp.expm1(2.0 * log_a)) * (i * xc).astype(jnp.float32)

    def combine(p, q):
        a1, b1 = p
        a2, b2 = q
        return a1 * a2, a2 * b1 + b2

    a_cum, b_cum = lax.associative_scan(combine, (a, bx), axis=1)
    h = b_cum if h0 is None else a_cum * h0[:, None, :] + b_cum
    return h, h[:, -1]

def rglru_direction(x_lat, x_ctx, conv_w, conv_b, w_r, b_r, w_i, b_i, lam, reverse):
    if reverse:
        x_lat, x_ctx = jnp.flip(x_lat, 1), jnp.flip(x_ctx, 1)
    h_ctx, h_last = rglru_scan(x_ctx, None, conv_w, conv_b, w_r, b_r, w_i, b_i, lam)
    h_lat, _ = rglru_scan(x_lat, h_last, conv_w, conv_b, w_r, b_r, w_i, b_i, lam)
    if reverse:
        h_lat, h_ctx = jnp.flip(h_lat, 1), jnp.flip(h_ctx, 1)
    return h_lat.astype(x_lat.dtype), h_ctx.astype(x_ctx.dtype)

def window_attention(q, k, v, k_ctx, v_ctx, sink):
    B, L = q.shape[:2]
    nb = L // Q_BLOCK
    qb = q.reshape(B, nb, Q_BLOCK, N_KV_HEADS, GQA_GROUP, HEAD_DIM)

    def bands(t):
        tp = jnp.pad(t, ((0, 0), (Q_BLOCK, Q_BLOCK), (0, 0), (0, 0)))
        tp = tp.reshape(B, nb + 2, Q_BLOCK, N_KV_HEADS, HEAD_DIM)
        return jnp.concatenate([tp[:, :-2], tp[:, 1:-1], tp[:, 2:]], axis=2)

    kb, vb = bands(k), bands(v)
    scale = HEAD_DIM ** -0.5
    s_loc = jnp.einsum("bnqkgd,bnskd->bnkgqs", qb, kb, preferred_element_type=jnp.float32) * scale
    s_ctx = jnp.einsum("bnqkgd,bskd->bnkgqs", qb, k_ctx, preferred_element_type=jnp.float32) * scale
    qi = jnp.arange(Q_BLOCK)[:, None]
    kj = jnp.arange(3 * Q_BLOCK)[None, :]
    rel = kj - Q_BLOCK - qi
    kpos = jnp.arange(nb)[:, None, None] * Q_BLOCK - Q_BLOCK + kj[None]
    valid = (jnp.abs(rel) <= WINDOW)[None] & (kpos >= 0) & (kpos < L)
    s_loc = jnp.where(valid[None, :, None, None], s_loc, -jnp.inf)
    sink_b = sink.astype(jnp.float32).reshape(N_KV_HEADS, GQA_GROUP, 1, 1)
    p = sink_softmax(jnp.concatenate([s_loc, s_ctx], axis=-1), sink_b)
    p_loc = p[..., :3 * Q_BLOCK].astype(v.dtype)
    p_ctx = p[..., 3 * Q_BLOCK:].astype(v.dtype)
    out = jnp.einsum("bnkgqs,bnskd->bnqkgd", p_loc, vb) + jnp.einsum("bnkgqs,bskd->bnqkgd", p_ctx, v_ctx)
    return out.reshape(B, L, D_ATTN).astype(q.dtype)

def context_attention(q_ctx, k_ctx, v_ctx, sink):
    B, Lc = q_ctx.shape[:2]
    qg = q_ctx.reshape(B, Lc, N_KV_HEADS, GQA_GROUP, HEAD_DIM)
    s = jnp.einsum("bqkgd,bskd->bkgqs", qg, k_ctx, preferred_element_type=jnp.float32) * HEAD_DIM ** -0.5
    p = sink_softmax(s, sink.astype(jnp.float32).reshape(N_KV_HEADS, GQA_GROUP, 1, 1)).astype(v_ctx.dtype)
    return jnp.einsum("bkgqs,bskd->bqkgd", p, v_ctx).reshape(B, Lc, D_ATTN)

def mixer_layer(x, xc, c_act, cc_act, norm_g, w_ada, b_ada, w_in, dw_w, dw_b, ln_g, ln_b, pw_w, pw_b,
                lru_conv_w, lru_conv_b, lru_w_r, lru_b_r, lru_w_i, lru_b_i, lru_lam, sink, w_out,
                cos, sin, last):
    B, L, _ = x.shape
    Lc = xc.shape[1]
    h, gate = modulate(x, norm_g, (c_act @ w_ada + b_ada)[:, None, :])
    hc, gate_c = modulate(xc, norm_g, cc_act @ w_ada + b_ada)
    u = h @ w_in
    uc = hc @ (w_in[:, :OFF_MEM_END] if last else w_in)

    q = apply_axial_rope(u[..., OFF_Q:OFF_ATTN_GATE].reshape(B, L, N_Q_HEADS, HEAD_DIM), cos, sin)
    k = apply_axial_rope(u[..., OFF_K:OFF_V].reshape(B, L, N_KV_HEADS, HEAD_DIM), cos, sin)
    v = u[..., OFF_V:OFF_MEM_END].reshape(B, L, N_KV_HEADS, HEAD_DIM)
    k_ctx = uc[..., OFF_K:OFF_V].reshape(B, Lc, N_KV_HEADS, HEAD_DIM)
    v_ctx = uc[..., OFF_V:OFF_MEM_END].reshape(B, Lc, N_KV_HEADS, HEAD_DIM)

    y_lru, y_lru_c = None, None
    for d in range(2):
        hl, hcx = rglru_direction(u[..., OFF_LRU_X:OFF_K], uc[..., OFF_LRU_X:OFF_K],
                                  lru_conv_w[d], lru_conv_b[d], lru_w_r[d], lru_b_r[d],
                                  lru_w_i[d], lru_b_i[d], lru_lam[d], reverse=(d == 1))
        y_lru = hl if y_lru is None else y_lru + hl
        y_lru_c = hcx if y_lru_c is None else y_lru_c + hcx

    y_conv = conv_branch(u[..., OFF_CONV_GLU:OFF_CONV_GATE], u[..., OFF_CONV_GATE:OFF_LRU_GATE],
                         dw_w, dw_b, ln_g, ln_b, pw_w, pw_b)
    y_lru = y_lru * jax.nn.silu(u[..., OFF_LRU_GATE:OFF_Q])
    y_attn = window_attention(q, k, v, k_ctx, v_ctx, sink) * jax.nn.silu(u[..., OFF_ATTN_GATE:D_IN])
    x = x + gate * (jnp.concatenate([y_conv, y_lru, y_attn], axis=-1) @ w_out)

    if not last:
        q_ctx = uc[..., OFF_Q:OFF_ATTN_GATE].reshape(B, Lc, N_Q_HEADS, HEAD_DIM)
        yc_conv = conv_branch(uc[..., OFF_CONV_GLU:OFF_CONV_GATE], uc[..., OFF_CONV_GATE:OFF_LRU_GATE],
                              dw_w, dw_b, ln_g, ln_b, pw_w, pw_b)
        yc_lru = y_lru_c * jax.nn.silu(uc[..., OFF_LRU_GATE:OFF_Q])
        yc_attn = context_attention(q_ctx, k_ctx, v_ctx, sink) * jax.nn.silu(uc[..., OFF_ATTN_GATE:D_IN])
        xc = xc + gate_c * (jnp.concatenate([yc_conv, yc_lru, yc_attn], axis=-1) @ w_out)
    return x, xc

def setup_inputs(seed: int = 0) -> dict:
    key = jax.random.key(seed)
    ks = jax.random.split(key, 24)
    f32 = jnp.float32

    def nrm(k, shape, s):
        return jax.random.normal(k, shape, f32) * s

    a0 = jax.random.uniform(ks[20], (DEPTH, 2, D_LRU), f32, 0.9, 0.999)
    return {
        "x": nrm(ks[0], (BATCH, SEQ, D_MODEL), 1.0),
        "c": nrm(ks[1], (BATCH, D_MODEL), 1.0),
        "ctx": nrm(ks[2], (BATCH, CTX_LEN, D_MODEL), 1.0),
        "c_ctx": nrm(ks[3], (D_MODEL,), 1.0),
        "norm_g": 1.0 + nrm(ks[4], (DEPTH, D_MODEL), 0.02),
        "w_ada": nrm(ks[5], (DEPTH, D_MODEL, 3 * D_MODEL), 0.5 * D_MODEL ** -0.5),
        "b_ada": nrm(ks[6], (DEPTH, 3 * D_MODEL), 0.02),
        "w_in": nrm(ks[7], (DEPTH, D_MODEL, D_IN), D_MODEL ** -0.5),
        "dw_w": nrm(ks[8], (DEPTH, CONV_WIDTH, D_CONV), CONV_WIDTH ** -0.5),
        "dw_b": nrm(ks[9], (DEPTH, D_CONV), 0.02),
        "ln_g": 1.0 + nrm(ks[10], (DEPTH, D_CONV), 0.02),
        "ln_b": nrm(ks[11], (DEPTH, D_CONV), 0.02),
        "pw_w": nrm(ks[12], (DEPTH, D_CONV, D_CONV), D_CONV ** -0.5),
        "pw_b": nrm(ks[13], (DEPTH, D_CONV), 0.02),
        "lru_conv_w": nrm(ks[14], (DEPTH, 2, LRU_CONV_WIDTH, D_LRU), LRU_CONV_WIDTH ** -0.5),
        "lru_conv_b": nrm(ks[15], (DEPTH, 2, D_LRU), 0.02),
        "lru_w_r": nrm(ks[16], (DEPTH, 2, LRU_BLOCKS, LRU_BLOCK, LRU_BLOCK), LRU_BLOCK ** -0.5),
        "lru_b_r": nrm(ks[17], (DEPTH, 2, D_LRU), 0.02),
        "lru_w_i": nrm(ks[18], (DEPTH, 2, LRU_BLOCKS, LRU_BLOCK, LRU_BLOCK), LRU_BLOCK ** -0.5),
        "lru_b_i": nrm(ks[19], (DEPTH, 2, D_LRU), 0.02),
        "lru_lam": jnp.log(a0) - jnp.log1p(-a0),
        "attn_sink": nrm(ks[21], (DEPTH, N_Q_HEADS), 1.0),
        "w_out": nrm(ks[22], (DEPTH, D_MIX, D_MODEL), D_MIX ** -0.5),
        "final_g": 1.0 + nrm(ks[23], (D_MODEL,), 0.02),
    }

def reference(x, c, ctx, c_ctx, norm_g, w_ada, b_ada, w_in, dw_w, dw_b, ln_g, ln_b, pw_w, pw_b,
              lru_conv_w, lru_conv_b, lru_w_r, lru_b_r, lru_w_i, lru_b_i, lru_lam, attn_sink,
              w_out, final_g):
    cos, sin = axial_rope_tables(x.shape[1])
    c_act = jax.nn.silu(c)
    cc_act = jax.nn.silu(c_ctx)
    xc = ctx
    for l in range(DEPTH):
        x, xc = mixer_layer(x, xc, c_act, cc_act, norm_g[l], w_ada[l], b_ada[l], w_in[l],
                            dw_w[l], dw_b[l], ln_g[l], ln_b[l], pw_w[l], pw_b[l],
                            lru_conv_w[l], lru_conv_b[l], lru_w_r[l], lru_b_r[l],
                            lru_w_i[l], lru_b_i[l], lru_lam[l], attn_sink[l], w_out[l],
                            cos, sin, last=(l == DEPTH - 1))
    return rmsnorm(x, final_g)


_drawn_inputs = setup_inputs


def setup_inputs(seed=0):
    import zlib

    import numpy as np

    out = dict(_drawn_inputs(seed))
    spreads = {}
    factors = {'ctx': 2.679,
     'norm_g': 8.0,
     'b_ada': 3.052,
     'dw_b': 8.0,
     'ln_g': 8.0,
     'ln_b': 8.0,
     'pw_b': 8.0,
     'lru_conv_b': 5.924,
     'lru_b_r': 8.0,
     'lru_b_i': 8.0,
     'attn_sink': 8.0,
     'final_g': 2.881}
    for name, (base, spread) in spreads.items():
        noise = np.random.default_rng([zlib.crc32(name.encode()), seed]).standard_normal(out[name].shape)
        drawn = base * np.exp(spread * noise) if base else spread * noise
        out[name] = __import__('jax').numpy.asarray(drawn.astype(out[name].dtype))
    for name, factor in factors.items():
        out[name] = (out[name] * factor).astype(out[name].dtype)
    return out
```

```python
from contextlib import ExitStack

import numpy as np
import concourse.bass as bass
from concourse import mybir

F32 = mybir.dt.float32
F32R = mybir.dt.float32r
ACT = mybir.ActivationFunctionType
ALU = mybir.AluOpType
AX = mybir.AxisListType

P = 128
D = 2048
DT = D // P
LAT, CTX = 256, 256
TOK = LAT + CTX
LAYERS = 2
HD = 128
HEADS, KV_HEADS, GROUP = 8, 2, 4
SCALE = HD ** -0.5
QB = 128
TAPS = 31
PAD = TAPS // 2
LTAPS = 4
CT = 4
EPS = 1e-6
ADA_KINDS = 3
SHIFT, SCL, GATE = range(3)
MASKED = -1e30

BLOCKS = ([("x", t) for t in range(CT)] + [("k", i) for i in range(KV_HEADS)] + [("v", i) for i in range(KV_HEADS)]
          + [(s, t) for t in range(CT) for s in ("b", "a")]
          + [("q", h) for h in range(4)] + [("ag", h) for h in range(4)]
          + [("q", h) for h in range(4, 8)] + [("ag", h) for h in range(4, 8)]
          + [("lg", t) for t in range(CT)] + [("cg", t) for t in range(CT)]
          + [("out", m) for m in range(DT)])
NB = len(BLOCKS)
B_OUT = NB - DT
COLUMN = {"x": 0, "k": 512, "v": 768, "a": 1024, "b": 1536, "cg": 2048, "lg": 2560, "q": 3072, "ag": 4096}
BOTH = 8

LRU_AT = [4 + 3 * t for t in range(CT)]
CONV_AT, CONV_STEPS = 16, 6
LN_AT = 29
PW_AT = 33


def groups(l):
    if l == 0:
        out, s = {}, 22
        for kv in range(KV_HEADS):
            for ctx in (False, True):
                for qb in range(2):
                    out[s] = (kv, qb, ctx)
                    s += 2
        return out
    return {22: (0, 0, False), 25: (0, 1, False), 30: (1, 0, False), 33: (1, 1, False)}


def out_steps():
    return range(B_OUT, NB)


SMALL = [("c", DT * 2), ("ident", P), ("ones", P), ("perm", P), ("cos", LAT), ("sin", LAT), ("mask", 2 * P),
         ("norm_g", LAYERS * DT), ("final_g", DT), ("b_ada", LAYERS * ADA_KINDS * DT), ("dw_w", LAYERS * CT * TAPS),
         ("dw_b", LAYERS * CT), ("ln_g", LAYERS * CT), ("ln_b", LAYERS * CT), ("pw_b", LAYERS * CT),
         ("lcw", LAYERS * 2 * CT * LTAPS), ("lcb", LAYERS * 2 * CT), ("b_r", LAYERS * 2 * CT),
         ("b_i", LAYERS * 2 * CT), ("lam", LAYERS * 2 * CT), ("sink", LAYERS * HEADS)]
N_SMALL = sum(n for _, n in SMALL)


def ada_plan():
    rest = [(0, GATE, k) for k in range(DT)] + [(1, kind, k) for kind in (SHIFT, SCL, GATE) for k in range(DT)]
    plan = {}
    for b in range(NB):
        n = len(rest) - (NB - b - 1) if b < 8 else 1
        n = 2 if b < 8 else 1
        plan[b] = [rest.pop(0) for _ in range(min(n, len(rest)))]
    assert not rest
    return plan


def stream():
    plan = ada_plan()
    s = [("ada", 0, kind, k) for kind in (SCL, SHIFT) for k in range(DT)] + [("w", 0), ("w", 1)]
    for gb in range(LAYERS * NB):
        l, b = divmod(gb, NB)
        if b == PW_AT:
            s.append(("pw", l))
        if gb + 2 < LAYERS * NB:
            s.append(("w", gb + 2))
        if l == 0:
            s += [("ada", *a) for a in plan[b]]
    return s


class Counts:

    def __init__(self, nc, ctx, known):
        self.nc, self.ctx, self.known = nc, ctx, known
        self.sems, self.n, self.marks = {}, {}, {}

    def sem(self, name):
        if name not in self.sems:
            self.sems[name] = self.ctx.enter_context(self.nc.semaphore(name))
            self.n[name] = 0
        return self.sems[name]

    def up(self, name, *key, by=1):
        s = self.sem(name)
        self.n[name] += by
        self.marks[(name, *key)] = self.n[name]
        return s, by

    def at(self, name, *key):
        return self.sem(name), self.known.get((name, *key), 1)

    def ago(self, name, n=0):
        return self.sem(name), self.n[name] - n


def program(nc, io, known):
    ctx = ExitStack()
    with ctx:
        def sb(name, shape, dt=F32):
            return ctx.enter_context(nc.sbuf_tensor(name, shape, dt))

        def pb(name, shape):
            return ctx.enter_context(nc.psum_tensor(name, shape, F32))

        NRAW = 3
        hh = sb("h_hi", [P, DT, TOK], F32R)
        hl = sb("h_lo", [P, DT, TOK], F32R)
        Y = sb("Y", [P, DT, TOK])
        raw = sb("raw", [P, NRAW, DT * P])
        wh = sb("w_hi", [P, 4, DT // 2 * P], F32R)
        wl = sb("w_lo", [P, 4, DT // 2 * P], F32R)
        T = sb("T", [P, 8, TOK])
        glu = sb("glu", [P, CT, 2, PAD + LAT + PAD])
        qreg = sb("qreg", [P, HEADS * TOK])
        kT = sb("kT", [P, KV_HEADS, TOK])
        v = sb("v", [P, 4, KV_HEADS * HD])
        bd = sb("bd", [P, 2, 2 * CT, P])
        tbuf = sb("tbuf", [P, TOK])
        lnr = sb("lnr", [P, TOK])
        cstat = sb("cstat", [P, DT, 32])
        adasb = lnr
        small = sb("small", [P, N_SMALL])
        der = sb("der", [P, LAYERS * (2 * 2 * CT + 2 * CT + HEADS)])
        ada = sb("ada", [P, LAYERS, 2, ADA_KINDS * DT])
        A = sb("A", [P, LAYERS, 2, DT])
        st = sb("stats", [P, 6, 4])
        eps = sb("eps", [P, 1])
        tiny = sb("tiny", [P, 3, 32])

        pB = [pb(f"psum_block{i}", [P, TOK]) for i in range(2)]
        psA = pb("psum_ada", [P, TOK])
        psM = pb("psum_misc", [P, TOK])
        psS = pb("psum_scores", [P, 4, TOK])

        q = qreg[:, :].rearrange("p (h t) -> p h t", h=HEADS)
        LW = LTAPS - 1 + LAT + LTAPS - 1
        lrux = qreg[:, HEADS * TOK - CT * 2 * LW:].rearrange("p (t s w) -> p t s w", t=CT, s=2)

        at = {}
        o = 0
        for name, n in SMALL:
            at[name] = small[:, o:o + n]
            o += n
        cT = at["c"].rearrange("p (k v) -> p k v", v=2)
        ident, ones, perm = at["ident"], at["ones"], at["perm"]
        cos, sin = at["cos"], at["sin"]
        mask = at["mask"].rearrange("p (m k) -> p m k", m=2)
        norm_g = at["norm_g"].rearrange("p (l k) -> p l k", l=LAYERS)
        b_ada = at["b_ada"].rearrange("p (l k) -> p l k", l=LAYERS)
        lcw = at["lcw"].rearrange("p (n k) -> p n k", k=LTAPS)
        sink = at["sink"]

        d0 = [0]

        def cut(n):
            d0[0] += n
            return der[:, d0[0] - n:d0[0]]

        dwh = at["dw_w"]
        hbr, hbi = at["b_r"], at["b_i"]
        s4n, s4 = cut(LAYERS * 2 * CT), cut(LAYERS * 2 * CT)
        lnhg, lnhb = cut(LAYERS * CT), cut(LAYERS * CT)
        nsink = cut(LAYERS * HEADS)

        C = Counts(nc, ctx, known)
        STREAM = stream()
        where = {s: i for i, s in enumerate(STREAM)}
        PLAN = ada_plan()
        GLOB = LAYERS * NB

        def arrived(item):
            i = where[item]
            return C.sem(f"raw{i % NRAW}"), 16 * (i // NRAW + 1)

        def raw_of(item):
            return raw[:, where[item] % NRAW, :]

        def width(l, b):
            return TOK if l == 0 or b < BOTH else LAT

        def Yv(l, m):
            return Y[:, m, :] if l == 0 else Y[:, m, LAT:TOK]

        def segs(ap):
            return ap.rearrange("p (s t) -> p s t", t=LAT)

        def glu_in(l, t):
            return glu[:, t, 0:(2 if l == 0 else 1), PAD:PAD + LAT]

        def released(gb):
            kind = BLOCKS[gb % NB][0]
            return C.at("evac_act" if kind in "xkvbq" else "evac_dve", gb)

        def pw_bank(l, m):
            return psM if m % 2 == 0 else pB[(l * NB + PW_AT + 1) % 2]

        def conv_taps(b):
            j = b - CONV_AT
            if not 0 <= j < 2 * CONV_STEPS:
                return []
            pair, j = divmod(j, CONV_STEPS)
            lo, hi = TAPS * j // CONV_STEPS, TAPS * (j + 1) // CONV_STEPS
            return [(2 * pair + i, k) for k in range(lo, hi) for i in range(2)]

        block = ctx.enter_context(nc.Block())

        @block.sync
        def _(sp):
            sp.dma_start(small[:, :], io["small"]).then_inc(*C.up("small_in", by=16))

            def gate_weights(l):
                if l:
                    sp.wait_ge(*C.at("lru_mm", l - 1, CT - 1))
                else:
                    sp.wait_ge(*C.at("bd_zero"))
                for g in range(2):
                    for j in range(2):
                        sp.dma_start(bd[64 * j:64 * j + 64, g, :, 64 * j:64 * j + 64],
                                     io["lru_w"][l, g, j]).then_inc(*C.up("bd_in", l, g, j, by=16))

            def residual(m):
                if m < 2:
                    sp.wait_ge(*C.at("att_out", 0, max(groups(0))))
                else:
                    sp.wait_ge(*C.at("evac_dve", B_OUT + m - 2))
                sp.dma_start(T[:, m % 2, :], io["xT"][:, m, :]).then_inc(*C.up(f"xs{m % 2}", m, by=16))

            for i, item in enumerate(STREAM):
                if i >= NRAW:
                    old = STREAM[i - NRAW]
                    if old[0] == "w":
                        sp.wait_ge(*C.at("lo", 2 * old[1] + 1))
                    elif old[0] == "ada":
                        sp.wait_ge(*C.at("ada_mm", *old[1:]))
                    else:
                        sp.wait_ge(*C.at("pw_mm", old[1], CT - 1))
                if item[0] == "w":
                    src = io["w_blocks"][item[1]]
                elif item[0] == "pw":
                    src = io["pw"][item[1]]
                else:
                    l, kind, k = item[1:]
                    src = io["w_ada"][l, k * P:(k + 1) * P, kind * D:(kind + 1) * D]
                sp.dma_start(raw[:, i % NRAW, :], src).then_inc(C.sem(f"raw{i % NRAW}"), 16)
                if i == NRAW:
                    sp.dma_start(Y[:, :, :], io["xT"]).then_inc(*C.up("x_in", by=16))
                if i == 2 * DT:
                    gate_weights(0)
                if item == ("w", B_OUT):
                    gate_weights(1)
                if item[0] == "w" and 0 <= item[1] - B_OUT - 2 < DT:
                    residual(item[1] - B_OUT - 2)
            for m in range(0, DT, 4):
                sp.wait_ge(*C.at("final", m + 3))
                sp.dma_start(io["out"][:, m:m + 4, :], Y[:, m:m + 4, 0:LAT]).then_inc(*C.up("stored", by=16))
            sp.wait_ge(*C.ago("stored"))

        @block.gpsimd
        def _(pool):
            nc.gpsimd.memset(cstat[:, :, :], 0.0).then_inc(*C.up("cstat_zero"))
            nc.gpsimd.memset(eps[:, :], EPS).then_inc(*C.up("eps_set"))
            nc.gpsimd.memset(bd[:, :, :, :], 0.0).then_inc(*C.up("bd_zero"))
            nc.gpsimd.memset(glu[:, :, :, :], 0.0).then_inc(*C.up("glu_zero"))
            for l in range(LAYERS):
                if l:
                    pool.wait_ge(*C.at("scores", l - 1, max(groups(l - 1))))
                nc.gpsimd.memset(lrux[:, :, :, :], 0.0).then_inc(*C.up("lrux_zero", l))

        @block.tensor
        def _(pe):
            mm = nc.tensor.matmul

            def ada_mm(l, kind, k):
                pe.wait_ge(*arrived(("ada", l, kind, k)))
                w = raw_of(("ada", l, kind, k))
                if k == 0 and (l, kind) != (0, SCL):
                    pe.wait_ge(*C.ago("ada_tp"))
                    pe.wait_ge(*C.at("ada_out", *before(l, kind)))
                for j in range(4):
                    last = mm(psA[32 * j:32 * j + 32, :], cstat[:, k, :], w[:, j * TOK:(j + 1) * TOK],
                              start=(k == 0), stop=(k == DT - 1), tile_position=(0, 32 * j))
                last.then_inc(*C.up("ada_mm", l, kind, k))

            def ada_tp(l, kind):
                pe.wait_ge(*C.at("ada_rows", l, kind))
                for j in range(4):
                    last = nc.tensor.transpose(psA[:, j * P:(j + 1) * P], adasb[:, j * P:(j + 1) * P], ident)
                last.then_inc(*C.up("ada_tp", l, kind))

            def rms_mm(l, m):
                n = TOK if l < LAYERS else LAT
                pe.wait_ge(*C.at("rms_sq", l, m))
                mm(psS[:, 0, 0:n], ones, T[:, 2 + m % 2, 0:n], start=(m == 0), stop=(m == DT - 1)
                   ).then_inc(*C.up("rms_mm", l, m))

            def mm_half(gb, j):
                l, b = divmod(gb, NB)
                n = width(l, b)
                ps = pB[gb % 2]
                pe.wait_ge(*C.at("lo", 2 * gb + j))
                if j == 0 and b == PW_AT + 1:
                    pe.wait_ge(*C.at("pw_out", l, CT - 1))
                elif j == 0 and gb >= 2:
                    pe.wait_ge(*released(gb - 2))
                slot = (2 * gb + j) % 4
                for i in range(DT // 2):
                    k = j * DT // 2 + i
                    if b == 0:
                        pe.wait_ge(*C.at("h_lo", l, k))
                    elif b == B_OUT:
                        pe.wait_ge(*C.at("y_lo", l, k))
                    hi, lo = wh[:, slot, i * P:(i + 1) * P], wl[:, slot, i * P:(i + 1) * P]
                    mm(ps[:, 0:n], hi, hh[:, k, 0:n], start=(k == 0), stop=False)
                    mm(ps[:, 0:n], hi, hl[:, k, 0:n], start=False, stop=False)
                    last = mm(ps[:, 0:n], lo, hh[:, k, 0:n], start=False, stop=(k == DT - 1))
                last.then_inc(*C.up("mm", 2 * gb + j))

            def rope_mm(l, b):
                kind, i = BLOCKS[b]
                pe.wait_ge(*C.at("evac_act", l * NB + b))
                misc_free(l)
                src = kT[:, i, 0:LAT] if kind == "k" else q[:, i, 0:LAT]
                mm(psM[:, 0:LAT], perm, src, start=True, stop=True).then_inc(*C.up("rope_mm", l, kind, i))

            def misc_free(l):
                if misc:
                    pe.wait_ge(*C.at(*misc[-1]))

            misc = []
            scores_free = []

            def lru_mm(l, t):
                pe.wait_ge(*C.at("taps", l, t, 1))
                if t == 0:
                    pe.wait_ge(*C.at("bd_in", l, 1, 1))
                    pe.wait_ge(*C.at("rms_std", l))
                else:
                    pe.wait_ge(*C.at("lru_tanh", l, t - 1, 1))
                for d in range(2):
                    for g in range(2):
                        last = mm(psS[:, 2 * d + g, :], bd[:, g, d * CT + t, :], T[:, 4 * d, :], start=True, stop=True)
                last.then_inc(*C.up("lru_mm", l, t))

            def scores(l, s):
                kv, qb, isctx = groups(l)[s]
                pe.wait_ge(*C.at("rope", l, "k", KV_HEADS - 1))
                if isctx:
                    pe.wait_ge(*C.at("evac_act", l * NB + 16 + 8 * kv + 3))
                else:
                    pe.wait_ge(*C.at("rope", l, "q", GROUP * kv + GROUP - 1))
                if scores_free:
                    pe.wait_ge(*C.at("att_out", l, scores_free[-1]))
                else:
                    pe.wait_ge(*C.at("lru_tanh", l, CT - 1, 1))
                t0 = (LAT if isctx else 0) + qb * QB
                for g in range(GROUP):
                    qt = q[:, GROUP * kv + g, t0:t0 + QB]
                    if isctx:
                        last = mm(psS[:, g, LAT:TOK], qt, kT[:, kv, LAT:TOK], start=True, stop=True)
                    else:
                        mm(psS[:, g, :], qt, kT[:, kv, :], start=True, stop=False)
                        far = (1 - qb) * QB
                        last = mm(psS[:, g, far:far + QB], ident, mask[:, qb, :], start=False, stop=True)
                last.then_inc(*C.up("scores", l, s))
                scores_free.append(s)

            def p_tp(l, s):
                isctx = groups(l)[s][2]
                for g in range(GROUP):
                    pe.wait_ge(*C.at("probs", l, s, g))
                    for kt in range(2 if isctx else 0, 4):
                        last = nc.tensor.transpose(psS[:, g, kt * P:(kt + 1) * P], T[:, g, kt * P:(kt + 1) * P], ident)
                    last.then_inc(*C.up("p_tp", l, s, g))

            def pv(l, s):
                kv, qb, isctx = groups(l)[s]
                pe.wait_ge(*C.at("pT", l, s, GROUP - 1))
                pe.wait_ge(*C.at("v_out", l, KV_HEADS - 1))
                first = 2 if isctx else 0
                for kt in range(first, 4):
                    last = mm(psS[:, 0, :], v[:, kt, kv * HD:(kv + 1) * HD], T[:, 4 + kt, :],
                              start=(kt == first), stop=(kt == 3))
                last.then_inc(*C.up("pv", l, s))

            def ln_mm(l, stage):
                n = TOK if l == 0 else LAT
                misc_free(l)
                if stage == "ln_sum":
                    for t in range(CT):
                        pe.wait_ge(*C.at("conv", l, t, TAPS - 1))
                        last = mm(psM[:, 0:n], ones, Yv(l, t), start=(t == 0), stop=(t == CT - 1))
                    misc.append(("ln_c", l, CT - 1))
                else:
                    for t in range(CT):
                        pe.wait_ge(*C.at("ln_sq", l, t))
                        last = mm(psM[:, 0:n] if l else segs(psM[:, 0:n]), ones, glu_in(l, t) if l == 0 else glu[:, t, 0, PAD:PAD + LAT],
                                  start=(t == 0), stop=(t == CT - 1))
                    misc.append(("ln_std", l))
                last.then_inc(*C.up(stage, l))

            def pw_mm(l, m):
                n = TOK if l == 0 else LAT
                if m < 2:
                    misc_free(l)
                    pe.wait_ge(*released(l * NB + PW_AT - 1))
                else:
                    pe.wait_ge(*C.at("pw_out", l, m - 2))
                if m == 0:
                    pe.wait_ge(*arrived(("pw", l)))
                w = raw_of(("pw", l)).rearrange("p (m k c) -> p m k c", m=CT, k=CT)
                for k in range(CT):
                    if m == 0:
                        pe.wait_ge(*C.at("ln_y", l, k))
                    last = mm(pw_bank(l, m)[:, 0:n], w[:, m, k, :], Yv(l, k), start=(k == 0), stop=(k == CT - 1))
                last.then_inc(*C.up("pw_mm", l, m))

            order = [(0, SCL), (0, SHIFT), (0, GATE), (1, SHIFT), (1, SCL), (1, GATE)]

            def before(l, kind):
                return order[order.index((l, kind)) - 1]

            pe.wait_ge(*C.at("small_in"))
            pe.wait_ge(*C.at("cstat", 1))
            for k in range(DT):
                ada_mm(0, SCL, k)
                rms_mm(0, k)
            ada_tp(0, SCL)
            for k in range(DT):
                ada_mm(0, SHIFT, k)
            ada_tp(0, SHIFT)

            for gb in range(GLOB):
                l, b = divmod(gb, NB)
                if b == 0:
                    scores_free.clear()
                    if l:
                        for m in range(DT - 2, DT):
                            rms_mm(l, m)
                mm_half(gb, 0)
                done = [a for a in (PLAN[b - 1] if l == 0 and b else PLAN[NB - 1] if b == 0 and l else []) if a[2] == DT - 1]
                for a in done:
                    ada_tp(*a[:2])
                if b - 2 in groups(l):
                    pv(l, b - 2)
                mm_half(gb, 1)
                if b and BLOCKS[b - 1][0] in "kq":
                    rope_mm(l, b - 1)
                    misc.append(("rope_t", l, *BLOCKS[b - 1]))
                if b and BLOCKS[b - 1][0] == "v":
                    i = BLOCKS[b - 1][1]
                    pe.wait_ge(*C.at("evac_act", gb - 1))
                    misc_free(l)
                    for kt in range(4):
                        last = nc.tensor.transpose(psM[:, kt * P:(kt + 1) * P], tbuf[:, kt * P:(kt + 1) * P], ident)
                    last.then_inc(*C.up("v_tp", l, i))
                    misc.append(("v_out", l, i))
                if b - 1 in LRU_AT:
                    lru_mm(l, LRU_AT.index(b - 1))
                if b in groups(l):
                    scores(l, b)
                if b - 1 in groups(l):
                    p_tp(l, b - 1)
                if b == LN_AT:
                    ln_mm(l, "ln_sum")
                if b == LN_AT + 1:
                    ln_mm(l, "ln_var")
                if b == PW_AT:
                    for m in range(CT):
                        pw_mm(l, m)
                    misc.append(("pw_out", l, CT - 1))
                if b - B_OUT >= 2:
                    rms_mm(l + 1, b - B_OUT - 2)
                if l == 0:
                    for a in PLAN[b]:
                        ada_mm(*a)
            for m in range(DT - 2, DT):
                rms_mm(LAYERS, m)

        @block.scalar
        def _(act):
            fn = nc.scalar.activation

            def hi(gb, j):
                act.wait_ge(*arrived(("w", gb)))
                if gb >= 2:
                    act.wait_ge(*C.at("mm", 2 * gb + j - 4))
                n = DT // 2 * P
                fn(wh[:, (2 * gb + j) % 4, :], raw_of(("w", gb))[:, j * n:(j + 1) * n], ACT.Copy
                   ).then_inc(*C.up("hi", 2 * gb + j))

            def ada_rows(l, kind):
                act.wait_ge(*C.at("ada_mm", l, kind, DT - 1))
                last_read = {(0, GATE): ("rope", 0, "k", 1), (1, SHIFT): ("rope", 0, "q", 3),
                             (1, SCL): ("ln_n", 0, CT - 1), (1, GATE): ("ln_n", 0, CT - 1)}.get((l, kind))
                if last_read:
                    act.wait_ge(*C.at(*last_read))
                fn(adasb[:, :], psA[:, :], ACT.Copy).then_inc(*C.up("ada_rows", l, kind))

            def square(l, m):
                n = TOK if l < LAYERS else LAT
                if l == 0:
                    if m == 0:
                        act.wait_ge(*C.at("x_in"))
                elif l:
                    act.wait_ge(*C.at("evac_dve", (l - 1) * NB + B_OUT + m))
                if m >= 2:
                    act.wait_ge(*C.at("rms_mm", l, m - 2))
                elif l:
                    act.wait_ge(*C.at("att_out", l - 1, max(groups(l - 1))))
                fn(T[:, 2 + m % 2, 0:n], Y[:, m, 0:n], ACT.Square).then_inc(*C.up("rms_sq", l, m))

            def rms_std(l):
                n = TOK if l < LAYERS else LAT
                act.wait_ge(*C.at("rms_mm", l, DT - 1))
                fn(tbuf[:, 0:n], psS[:, 0, 0:n], ACT.Sqrt, scale=1.0 / D, bias=eps[:, 0:1]).then_inc(*C.up("rms_std", l))

            def modulate(l, k):
                act.wait_ge(*C.at("mod", l, k, 1))
                for i in range(2):
                    fn(hh[:, k, i * LAT:(i + 1) * LAT], T[:, k % 2, i * LAT:(i + 1) * LAT], ACT.Identity,
                       bias=ada[:, l, i, SHIFT * DT + k:SHIFT * DT + k + 1]).then_inc(*C.up("h_hi", l, k, i))

            def evac(gb):
                l, b = divmod(gb, NB)
                kind, i = BLOCKS[b]
                n = width(l, b)
                if kind == "out":
                    return
                ps = pB[gb % 2][:, 0:n]
                act.wait_ge(*C.at("mm", 2 * gb + 1))
                if kind == "x":
                    act.wait_ge(*C.at("lrux_zero", l))
                    fn(lrux[:, i, :, LTAPS - 1:LTAPS - 1 + LAT], segs(ps), ACT.Copy).then_inc(*C.up("evac_act", gb))
                elif kind == "k":
                    fn(kT[:, i, :], ps, ACT.Copy).then_inc(*C.up("evac_act", gb))
                elif kind == "v":
                    if i:
                        act.wait_ge(*C.at("v_tp", l, i - 1))
                    fn(tbuf[:, :], ps, ACT.Copy).then_inc(*C.up("evac_act", gb))
                elif kind == "b":
                    if i == 0:
                        act.wait_ge(*C.at("v_tp", l, KV_HEADS - 1))
                    else:
                        act.wait_ge(*C.at("evac_dve", gb - 1))
                    fn(tbuf[:, 0:n], ps, ACT.Tanh, scale=0.5).then_inc(*C.up("evac_act", gb))
                elif kind == "q":
                    if i == 0:
                        act.wait_ge(*C.at("lru_h", l, CT - 1))
                    fn(q[:, i, 0:n], ps, ACT.Copy).then_inc(*C.up("evac_act", gb))
                elif kind == "ag":
                    fn(Yv(l, 8 + i), ps, ACT.Tanh, scale=0.5).then_inc(*C.up("gate_tanh", gb))
                elif kind in ("lg", "cg"):
                    if (kind, i) != ("lg", 0):
                        act.wait_ge(*C.at("evac_dve", gb - 1))
                    fn(tbuf[:, 0:n], ps, ACT.Tanh, scale=0.5).then_inc(*C.up("gate_tanh", gb))

            def lru_act(l, t):
                act.wait_ge(*C.at("lru_mm", l, t))
                for d in range(2):
                    c = (l * 2 + d) * CT + t
                    fn(T[:, 4 * d + 1, :], psS[:, 2 * d, :], ACT.Tanh, scale=0.5, bias=hbr[:, c:c + 1]
                       ).then_inc(*C.up("lru_tanh", l, t, d, "r"))
                    fn(T[:, 4 * d + 2, :], psS[:, 2 * d + 1, :], ACT.Tanh, scale=0.5, bias=hbi[:, c:c + 1]
                       ).then_inc(*C.up("lru_tanh", l, t, d))
                for d in range(2):
                    c = (l * 2 + d) * CT + t
                    act.wait_ge(*C.ago("lru_tanh", 2 - 2 * d + 1))
                    fn(T[:, 4 * d + 3, :], T[:, 4 * d + 1, :], ACT.Exp, scale=s4n[:, c:c + 1], bias=s4n[:, c:c + 1]
                       ).then_inc(*C.up("lru_a", l, t, d))
                for d in range(2):
                    c = (l * 2 + d) * CT + t
                    act.wait_ge(*C.ago("lru_a", 1 - d))
                    fn(T[:, 4 * d + 1, :], T[:, 4 * d + 1, :], ACT.Tanh, scale=s4[:, c:c + 1], bias=s4[:, c:c + 1]
                       ).then_inc(*C.up("lru_t", l, t, d))
                for d in range(2):
                    fn(q[:, d, :], T[:, 4 * d + 3, :], ACT.Square).then_inc(*C.up("lru_a2", l, t, d))

            def lru_sqrt(l, t):
                for d in range(2):
                    act.wait_ge(*C.at("lru_v", l, t, d))
                    fn(q[:, d, :], q[:, d, :], ACT.Sqrt, scale=0.25).then_inc(*C.up("lru_sq", l, t, d))

            def att_exp(l, s):
                kv, qb, isctx = groups(l)[s]
                k0 = LAT if isctx else 0
                act.wait_ge(*C.at("att_neg", l, s))
                if s != min(groups(l)):
                    act.wait_ge(*C.at("p_tp", l, max(x for x in groups(l) if x < s), GROUP - 1))
                for g in range(GROUP):
                    fn(T[:, g, k0:TOK], psS[:, g, k0:TOK], ACT.Exp, scale=SCALE, bias=st[:, 1, g:g + 1],
                       accum_out=st[:, 2, g:g + 1]).then_inc(*C.up("att_exp", l, s, g))
                act.wait_ge(*C.at("att_sn", l, s))
                fn(st[:, 4, :], st[:, 3, :], ACT.Exp).then_inc(*C.up("att_es", l, s))

            def att_pT(l, s):
                isctx = groups(l)[s][2]
                k0 = 2 if isctx else 0
                if s != min(groups(l)):
                    act.wait_ge(*C.at("pv", l, max(x for x in groups(l) if x < s)))
                for g in range(GROUP):
                    act.wait_ge(*C.at("p_tp", l, s, g))
                    fn(T[:, 4 + k0:8, g * QB:(g + 1) * QB],
                       psS[:, g, k0 * P:TOK].rearrange("p (k q) -> p k q", q=P), ACT.Copy).then_inc(*C.up("pT", l, s, g))

            act.wait_ge(*C.at("small_in"))
            fn(tiny[:, 0, :], at["c"], ACT.Tanh, scale=0.5).then_inc(*C.up("c_tanh"))
            n = LAYERS * 2 * CT
            fn(tiny[:, 1, 0:n], at["lam"], ACT.Abs).then_inc(*C.up("lam_abs"))
            act.wait_ge(*C.ago("lam_abs"))
            fn(tiny[:, 1, 0:n], tiny[:, 1, 0:n], ACT.Exp, scale=-1.0).then_inc(*C.up("lam_exp"))
            act.wait_ge(*C.at("lam_one"))
            fn(tiny[:, 2, 0:n], tiny[:, 1, 0:n], ACT.Ln).then_inc(*C.up("lam_ln"))
            act.wait_ge(*C.at("eps_set"))
            for k in range(DT):
                square(0, k)
            rms_std(0)
            ada_rows(0, SCL)
            for gb in range(2):
                for j in range(2):
                    if gb == 1 and j == 0:
                        ada_rows(0, SHIFT)
                    hi(gb, j)

            for gb in range(GLOB):
                l, b = divmod(gb, NB)
                if b == 0:
                    if l:
                        square(l, DT - 1)
                        rms_std(l)
                    for k in range(DT):
                        modulate(l, k)
                if b == B_OUT:
                    for k in range(DT):
                        if k == 0:
                            act.wait_ge(*C.at("mm", 2 * gb - 1))
                            act.wait_ge(*C.at("att_out", l, max(groups(l))))
                            act.wait_ge(*C.at("evac_dve", gb - 1))
                        n = width(l, b)
                        fn(hh[:, k, 0:n], Yv(l, k), ACT.Copy).then_inc(*C.up("y_hi", l, k))
                if gb + 2 < GLOB:
                    hi(gb + 2, 0)
                    hi(gb + 2, 1)
                evac(gb)
                if b and BLOCKS[b - 1][0] == "v":
                    i = BLOCKS[b - 1][1]
                    act.wait_ge(*C.at("v_tp", l, i))
                    fn(v[:, :, i * HD:(i + 1) * HD], psM[:, :].rearrange("p (k d) -> p k d", d=HD), ACT.Copy
                       ).then_inc(*C.up("v_out", l, i))
                if b - 2 in LRU_AT:
                    lru_sqrt(l, LRU_AT.index(b - 2))
                if b - 1 in LRU_AT:
                    lru_act(l, LRU_AT.index(b - 1))
                if b - 1 in groups(l):
                    att_pT(l, b - 1)
                if b in groups(l):
                    att_exp(l, b)
                if b == LN_AT:
                    for t in range(CT):
                        act.wait_ge(*C.at("ln_c", l, t))
                        fn(glu_in(l, t), segs(Yv(l, t)), ACT.Square).then_inc(*C.up("ln_sq", l, t))
                if b == LN_AT + 1:
                    n = width(l, b)
                    act.wait_ge(*C.at("ln_var", l))
                    fn(lnr[:, 0:n], psM[:, 0:n], ACT.Sqrt, scale=1.0 / (CT * P), bias=eps[:, 0:1]
                       ).then_inc(*C.up("ln_std", l))
                if b == LN_AT + 2:
                    for t in range(CT):
                        c = l * CT + t
                        act.wait_ge(*C.at("ln_n", l, t))
                        fn(glu_in(l, t), segs(Yv(l, t)), ACT.Tanh, scale=lnhg[:, c:c + 1], bias=lnhb[:, c:c + 1]
                           ).then_inc(*C.up("ln_th", l, t))
                for m in range(CT if b == PW_AT else 0):
                    n = width(l, b)
                    c = l * CT + m
                    act.wait_ge(*C.at("pw_mm", l, m))
                    if m == 0:
                        act.wait_ge(*C.at("ln_y", l, CT - 1))
                    fn(glu_in(l, m), segs(pw_bank(l, m)[:, 0:n]), ACT.Identity, scale=0.5, bias=at["pw_b"][:, c:c + 1]
                       ).then_inc(*C.up("pw_out", l, m))
                if b - B_OUT >= 1:
                    square(l + 1, b - B_OUT - 1)
                if l == 0:
                    for a in PLAN[b]:
                        if a[2] == DT - 1:
                            ada_rows(*a[:2])
            square(LAYERS, DT - 1)
            rms_std(LAYERS)

        @block.vector
        def _(dve):
            V = nc.vector
            stt = V.scalar_tensor_tensor

            def lo(gb, j):
                n = DT // 2 * P
                s = (2 * gb + j) % 4
                dve.wait_ge(*C.at("hi", 2 * gb + j))
                V.tensor_tensor(wl[:, s, :], raw_of(("w", gb))[:, j * n:(j + 1) * n], wh[:, s, :].bitcast(F32),
                                ALU.subtract).then_inc(*C.up("lo", 2 * gb + j))

            def ada_out(l, kind):
                dve.wait_ge(*C.at("ada_tp", l, kind))
                cols = psA[:, :].rearrange("p (q j r) -> p q j r", q=4, j=4)
                for i in range(2):
                    V.tensor_tensor(ada[:, l, i, kind * DT:(kind + 1) * DT].rearrange("p (j q) -> p q j", q=4),
                                    cols[:, :, :, i], b_ada[:, l, kind * DT:(kind + 1) * DT].rearrange("p (j q) -> p q j", q=4),
                                    ALU.add).then_inc(*C.up("ada_out", l, kind))
                if kind == SCL:
                    for i in range(2):
                        dve.wait_ge(*C.ago("ada_out", 0))
                        stt(A[:, l, i, :], ada[:, l, i, SCL * DT:(SCL + 1) * DT], 1.0, norm_g[:, l, :], ALU.add, ALU.mult
                            ).then_inc(*C.up("A", l, i))

            def modulate(l, k):
                for i in range(2):
                    w = slice(i * LAT, (i + 1) * LAT)
                    stt(T[:, k % 2, w], Y[:, k, w], A[:, l, i, k:k + 1], tbuf[:, w], ALU.mult, ALU.mult
                        ).then_inc(*C.up("mod", l, k, i))

            def h_lo(l, k):
                for i in range(2):
                    w = slice(i * LAT, (i + 1) * LAT)
                    dve.wait_ge(*C.at("h_hi", l, k, i))
                    stt(hl[:, k, w], T[:, k % 2, w], ada[:, l, i, SHIFT * DT + k:SHIFT * DT + k + 1],
                        hh[:, k, w].bitcast(F32), ALU.add, ALU.subtract).then_inc(*C.up("h_lo", l, k))

            def h_phase(l):
                dve.wait_ge(*C.at("rms_std", l))
                V.reciprocal(tbuf[:, :], tbuf[:, :]).then_inc(*C.up("rstd", l))
                if l == 0:
                    ada_out(0, SCL)
                    ada_out(0, SHIFT)
                dve.wait_ge(*C.ago("rstd"))
                dve.wait_ge(*C.ago("A"))
                dve.wait_ge(*C.ago("ada_out"))
                for k in range(DT):
                    if l and k < 2:
                        dve.wait_ge(*C.ago("evac_dve"))
                    if k >= 2:
                        dve.wait_ge(*C.ago("h_lo"))
                    modulate(l, k)
                    if k:
                        h_lo(l, k - 1)
                h_lo(l, DT - 1)

            def evac(gb):
                l, b = divmod(gb, NB)
                kind, i = BLOCKS[b]
                n = width(l, b)
                ps = pB[gb % 2][:, 0:n]
                if kind == "a":
                    dve.wait_ge(*C.at("mm", 2 * gb + 1))
                    dve.wait_ge(*C.at("evac_act", gb - 1))
                    dve.wait_ge(*C.at("glu_zero"))
                    stt(glu_in(l, i), segs(tbuf[:, 0:n]), 1.0, segs(ps), ALU.add, ALU.mult).then_inc(*C.up("evac_dve", gb))
                elif kind == "ag":
                    dve.wait_ge(*C.at("gate_tanh", gb))
                    stt(Yv(l, 8 + i), Yv(l, 8 + i), 1.0, ps, ALU.add, ALU.mult).then_inc(*C.up("evac_dve", gb))
                elif kind in ("lg", "cg"):
                    dve.wait_ge(*C.at("gate_tanh", gb))
                    stt(tbuf[:, 0:n], tbuf[:, 0:n], 1.0, ps, ALU.add, ALU.mult).then_inc(*C.up("gated", gb))
                    dve.wait_ge(*C.ago("gated"))
                    if kind == "lg":
                        stt(Yv(l, 4 + i), tbuf[:, 0:n], 0.5, Yv(l, 4 + i), ALU.mult, ALU.mult
                            ).then_inc(*C.up("evac_dve", gb))
                    else:
                        dve.wait_ge(*C.at("pw_out", l, i))
                        if i == 0:
                            dve.wait_ge(*C.at("pw_mm", l, CT - 1))
                        stt(segs(Yv(l, i)), segs(tbuf[:, 0:n]), 0.5, glu_in(l, i), ALU.mult, ALU.mult
                            ).then_inc(*C.up("evac_dve", gb))
                elif kind == "out":
                    dve.wait_ge(*C.at("mm", 2 * gb + 1))
                    if l == 0:
                        dve.wait_ge(*C.at(f"xs{i % 2}", i))
                    for s in range(n // LAT):
                        w = slice(s * LAT, (s + 1) * LAT)
                        old = T[:, i % 2, w] if l == 0 else Y[:, i, w]
                        stt(Y[:, i, w], ps[:, w], ada[:, l, s, GATE * DT + i:GATE * DT + i + 1], old, ALU.mult, ALU.add
                            ).then_inc(*C.up("evac_dve", gb))

            def rope(l, b):
                kind, i = BLOCKS[b]
                x = kT[:, i, 0:LAT] if kind == "k" else q[:, i, 0:LAT]
                dve.wait_ge(*C.at("rope_mm", l, kind, i))
                if (l, kind, i) != (0, "k", 0):
                    dve.wait_ge(*C.ago("rope"))
                V.tensor_tensor(lnr[:, 0:LAT], psM[:, 0:LAT], sin, ALU.mult).then_inc(*C.up("rope_t", l, kind, i))
                V.tensor_tensor(x, x, cos, ALU.mult).then_inc(*C.up("rope_c", l, kind, i))
                dve.wait_ge(*C.ago("rope_c"))
                V.tensor_tensor(x, x, lnr[:, 0:LAT], ALU.add).then_inc(*C.up("rope", l, kind, i))

            def taps(l, t):
                if t == 0:
                    dve.wait_ge(*C.ago("h_lo"))
                dve.wait_ge(*C.at("evac_act", l * NB + t))
                if t:
                    dve.wait_ge(*C.ago("lru_h"))
                for k in range(LTAPS):
                    for d in range(2):
                        c = (l * 2 + d) * CT + t
                        s = k if d == 0 else 2 * (LTAPS - 1) - k
                        x = lrux[:, t, :, s:s + LAT]
                        out = segs(T[:, 4 * d, :])
                        if k == 0:
                            V.tensor_scalar(out, x, lcw[:, c, 0:1], at["lcb"][:, c:c + 1], ALU.mult, ALU.add
                                            ).then_inc(*C.up("taps", l, t, d))
                        else:
                            dve.wait_ge(*C.ago("taps", 1))
                            stt(out, x, lcw[:, c, k:k + 1], out, ALU.mult, ALU.add).then_inc(*C.up("taps", l, t, d))

            def lru_v(l, t):
                for d in range(2):
                    dve.wait_ge(*C.at("lru_a2", l, t, d))
                    stt(q[:, d, :], q[:, d, :], 1.0, T[:, 4 * d + 1, :], ALU.add, ALU.mult).then_inc(*C.up("lru_v", l, t, d))
                for d in range(2):
                    stt(T[:, 4 * d + 2, :], T[:, 4 * d + 2, :], 1.0, T[:, 4 * d, :], ALU.add, ALU.mult
                        ).then_inc(*C.up("lru_g", l, t, d))

            def lru_scan(l, t):
                for d in range(2):
                    dve.wait_ge(*C.at("lru_sq", l, t, d))
                    dve.wait_ge(*C.ago("lru_g"))
                    V.tensor_tensor(T[:, 4 * d + 2, :], T[:, 4 * d + 2, :], q[:, d, :], ALU.mult
                                    ).then_inc(*C.up("lru_b", l, t, d))
                dve.wait_ge(*C.ago("lru_b", 1))
                f, r = T[:, 0, :], T[:, 4, :]
                V.tensor_tensor_scan(f[:, LAT:TOK], T[:, 3, LAT:TOK], T[:, 2, LAT:TOK], 0.0, ALU.mult, ALU.add
                                     ).then_inc(*C.up("lru_scan", l, t))
                dve.wait_ge(*C.ago("lru_b"))
                V.tensor_tensor_scan(r[:, ::-1], T[:, 7, ::-1], T[:, 6, ::-1], 0.0, ALU.mult, ALU.add
                                     ).then_inc(*C.up("lru_scan", l, t))
                dve.wait_ge(*C.ago("lru_scan", 1))
                V.tensor_tensor_scan(f[:, 0:LAT], T[:, 3, 0:LAT], T[:, 2, 0:LAT], f[:, TOK - 1:TOK], ALU.mult, ALU.add
                                     ).then_inc(*C.up("lru_scan", l, t))
                dve.wait_ge(*C.ago("lru_scan"))
                n = TOK if l == 0 else LAT
                V.tensor_tensor(Yv(l, 4 + t), f[:, 0:n], r[:, 0:n], ALU.add).then_inc(*C.up("lru_h", l, t))

            def conv(l, pairs):
                for t, k in pairs:
                    c = (l * CT + t) * TAPS + k
                    x = glu[:, t, 0:(2 if l == 0 else 1), k:k + LAT]
                    out = segs(Yv(l, t))
                    if k == 0:
                        dve.wait_ge(*C.ago("evac_dve"))
                        V.tensor_scalar(out, x, dwh[:, c:c + 1], at["dw_b"][:, l * CT + t:l * CT + t + 1], ALU.mult,
                                        ALU.add).then_inc(*C.up("conv", l, t, k))
                    else:
                        dve.wait_ge(*C.ago("conv", 1))
                        stt(out, x, dwh[:, c:c + 1], out, ALU.mult, ALU.add).then_inc(*C.up("conv", l, t, k))

            def att_max(l, s):
                kv, qb, isctx = groups(l)[s]
                k0 = LAT if isctx else 0
                h = l * HEADS + GROUP * kv
                dve.wait_ge(*C.at("scores", l, s))
                V.tensor_reduce(st[:, 0, :], psS[:, :, k0:TOK], axis=AX.X, op=ALU.max).then_inc(*C.up("att_max", l, s))
                dve.wait_ge(*C.ago("att_max"))
                stt(st[:, 1, :], st[:, 0, :], -SCALE, nsink[:, h:h + GROUP], ALU.mult, ALU.min).then_inc(*C.up("att_neg", l, s))
                dve.wait_ge(*C.ago("att_neg"))
                V.tensor_tensor(st[:, 3, :], st[:, 1, :], sink[:, h:h + GROUP], ALU.add).then_inc(*C.up("att_sn", l, s))

            def att_norm(l, s):
                isctx = groups(l)[s][2]
                k0 = LAT if isctx else 0
                dve.wait_ge(*C.at("att_es", l, s))
                V.tensor_tensor(st[:, 5, :], st[:, 2, :], st[:, 4, :], ALU.add).then_inc(*C.up("att_den", l, s))
                dve.wait_ge(*C.ago("att_den"))
                V.reciprocal(st[:, 5, :], st[:, 5, :]).then_inc(*C.up("att_den", l, s))
                dve.wait_ge(*C.ago("att_den"))
                for g in range(GROUP):
                    V.tensor_scalar(T[:, g, k0:TOK], T[:, g, k0:TOK], st[:, 5, g:g + 1], None, ALU.mult
                                    ).then_inc(*C.up("probs", l, s, g))

            def att_out(l, s):
                kv, qb, isctx = groups(l)[s]
                t0 = (LAT if isctx else 0) + qb * QB
                y = (Y if l == 0 else Y[:, :, LAT:TOK])[:, 8 + GROUP * kv:8 + GROUP * kv + GROUP, t0:t0 + QB]
                dve.wait_ge(*C.at("pv", l, s))
                stt(y, psS[:, 0, :].rearrange("p (g t) -> p g t", g=GROUP), 0.5, y, ALU.mult, ALU.mult
                    ).then_inc(*C.up("att_out", l, s))

            dve.wait_ge(*C.at("c_tanh"))
            stt(tiny[:, 0, :], tiny[:, 0, :], 1.0, at["c"], ALU.add, ALU.mult).then_inc(*C.up("cstat", 0))
            dve.wait_ge(*C.at("cstat_zero"))
            dve.wait_ge(*C.ago("cstat"))
            V.tensor_scalar(cstat[:, :, 0:2], tiny[:, 0, :].rearrange("p (k v) -> p k v", v=2), 0.5, None, ALU.mult
                            ).then_inc(*C.up("cstat", 1))
            n = LAYERS * 2 * CT
            dve.wait_ge(*C.at("lam_exp"))
            V.tensor_scalar(tiny[:, 1, 0:n], tiny[:, 1, 0:n], 1.0, None, ALU.add).then_inc(*C.up("lam_one"))
            V.tensor_scalar(tiny[:, 1, 16:16 + n], at["lam"], -1.0, 0.0, ALU.mult, ALU.max).then_inc(*C.up("derived"))
            dve.wait_ge(*C.at("lam_ln"))
            dve.wait_ge(*C.ago("derived"))
            V.tensor_tensor(tiny[:, 2, 0:n], tiny[:, 2, 0:n], tiny[:, 1, 16:16 + n], ALU.add).then_inc(*C.up("derived"))
            dve.wait_ge(*C.ago("derived"))
            for dst, src, f in ((s4, tiny[:, 2, 0:n], 4.0), (s4n, tiny[:, 2, 0:n], -4.0), (dwh, at["dw_w"], 0.5),
                                (hbr, at["b_r"], 0.5), (hbi, at["b_i"], 0.5), (lnhg, at["ln_g"], 0.5),
                                (lnhb, at["ln_b"], 0.5), (nsink, sink, -1.0)):
                V.tensor_scalar(dst, src, f, None, ALU.mult).then_inc(*C.up("derived"))
            dve.wait_ge(*C.ago("derived"))
            ada_first = True

            h_phase(0)
            for gb in range(2):
                for j in range(2):
                    lo(gb, j)

            for gb in range(GLOB):
                l, b = divmod(gb, NB)
                if b == 0 and l:
                    h_phase(l)
                if b == B_OUT:
                    n = width(l, b)
                    for k in range(DT):
                        dve.wait_ge(*C.at("y_hi", l, k))
                        V.tensor_tensor(hl[:, k, 0:n], Yv(l, k), hh[:, k, 0:n].bitcast(F32), ALU.subtract
                                        ).then_inc(*C.up("y_lo", l, k))
                if gb + 2 < GLOB:
                    lo(gb + 2, 0)
                    lo(gb + 2, 1)
                for a in (PLAN[b - 1] if l == 0 and b else PLAN[NB - 1] if b == 0 and l else []):
                    if a[2] == DT - 1:
                        ada_out(*a[:2])
                evac(gb)
                if b and BLOCKS[b - 1][0] in "kq":
                    rope(l, b - 1)
                if b - 2 in groups(l):
                    att_out(l, b - 2)
                if b in groups(l):
                    att_max(l, b)
                if b in LRU_AT:
                    pass
                if b - 1 in LRU_AT:
                    lru_v(l, LRU_AT.index(b - 1))
                if b - 2 in LRU_AT:
                    lru_scan(l, LRU_AT.index(b - 2))
                if b in LRU_AT:
                    taps(l, LRU_AT.index(b))
                conv(l, conv_taps(b))
                if b in groups(l):
                    att_norm(l, b)
                if b == LN_AT:
                    n = width(l, b)
                    dve.wait_ge(*C.at("ln_sum", l))
                    for t in range(CT):
                        stt(Yv(l, t), psM[:, 0:n], -1.0 / (CT * P), Yv(l, t), ALU.mult, ALU.add).then_inc(*C.up("ln_c", l, t))
                if b == LN_AT + 1:
                    n = width(l, b)
                    dve.wait_ge(*C.at("ln_std", l))
                    V.reciprocal(lnr[:, 0:n], lnr[:, 0:n]).then_inc(*C.up("ln_rstd", l))
                    dve.wait_ge(*C.ago("ln_rstd"))
                    for t in range(CT):
                        V.tensor_tensor(Yv(l, t), Yv(l, t), lnr[:, 0:n], ALU.mult).then_inc(*C.up("ln_n", l, t))
                if b == LN_AT + 2:
                    for t in range(CT):
                        c = l * CT + t
                        dve.wait_ge(*C.at("ln_th", l, t))
                        V.tensor_scalar(Yv(l, t), Yv(l, t), at["ln_g"][:, c:c + 1], at["ln_b"][:, c:c + 1], ALU.mult,
                                        ALU.add).then_inc(*C.up("ln_z", l, t))
                    for t in range(CT):
                        dve.wait_ge(*C.ago("ln_z", CT - 1 - t))
                        stt(segs(Yv(l, t)), glu_in(l, t), 1.0, segs(Yv(l, t)), ALU.add, ALU.mult).then_inc(*C.up("ln_y", l, t))

            dve.wait_ge(*C.at("rms_std", LAYERS))
            V.reciprocal(tbuf[:, 0:LAT], tbuf[:, 0:LAT]).then_inc(*C.up("rstd", LAYERS))
            dve.wait_ge(*C.ago("rstd"))
            dve.wait_ge(*C.ago("evac_dve"))
            for m in range(DT):
                stt(Y[:, m, 0:LAT], Y[:, m, 0:LAT], at["final_g"][:, m:m + 1], tbuf[:, 0:LAT], ALU.mult, ALU.mult
                    ).then_inc(*C.up("final", m))
        return dict(C.marks)


def _tables():
    ident = np.eye(P, dtype=np.float32)
    perm = np.zeros((P, P), np.float32)
    for m in range(P):
        perm[m + 32 if m % 64 < 32 else m - 32, m] = -1.0 if m % 64 < 32 else 1.0
    half = HD // 2
    inv = np.float32(10000.0) ** (-np.arange(0, half, 2, dtype=np.float32) / np.float32(half))
    t = np.arange(LAT)
    row, col = (t // 64).astype(np.float32), (t % 64).astype(np.float32)
    ang = np.concatenate([row[:, None] * inv, row[:, None] * inv, col[:, None] * inv, col[:, None] * inv], axis=1).T
    a, b = np.arange(P)[None, :], np.arange(P)[:, None]
    mask = np.stack([np.where(a > b, MASKED, 0.0), np.where(a < b, MASKED, 0.0)], axis=1).astype(np.float32)
    return {"ident": ident, "ones": np.ones((P, P), np.float32), "perm": perm,
            "cos": np.cos(ang).astype(np.float32), "sin": np.sin(ang).astype(np.float32), "mask": mask}


def _lay_out(x, c, ctx, c_ctx, norm_g, w_ada, b_ada, w_in, dw_w, dw_b, ln_g, ln_b, pw_w, pw_b, lru_conv_w,
             lru_conv_b, lru_w_r, lru_b_r, lru_w_i, lru_b_i, lru_lam, attn_sink, w_out, final_g):
    def cols(a):
        a = a.reshape(*a.shape[:-1], -1, P)
        return np.moveaxis(a, -1, 0).reshape(P, -1)

    small = _tables()
    small.update(
        c=np.stack([c[0].reshape(DT, P).T, c_ctx.reshape(DT, P).T], axis=2), norm_g=cols(norm_g), final_g=cols(final_g),
        b_ada=cols(b_ada), dw_w=np.moveaxis(dw_w.reshape(LAYERS, TAPS, CT, P), (3, 0, 2, 1), (0, 1, 2, 3)),
        dw_b=cols(dw_b), ln_g=cols(ln_g), ln_b=cols(ln_b), pw_b=cols(pw_b),
        lcw=lru_conv_w.reshape(LAYERS, 2, LTAPS, CT, P).transpose(4, 0, 1, 3, 2), lcb=cols(lru_conv_b),
        b_r=cols(lru_b_r), b_i=cols(lru_b_i), lam=cols(lru_lam),
        sink=np.broadcast_to(attn_sink.reshape(1, -1), (P, LAYERS * HEADS)))
    packed = np.concatenate([np.ascontiguousarray(small[name]).reshape(P, n) for name, n in SMALL], axis=1)
    blocks = []
    for l in range(LAYERS):
        for kind, i in BLOCKS:
            w, at = (w_out[l], i * P) if kind == "out" else (w_in[l], COLUMN[kind] + i * P)
            blocks.append(w[:, at:at + P].reshape(DT, P, P).transpose(1, 0, 2).reshape(P, DT * P))
    lru = np.stack([lru_w_r, lru_w_i], axis=1)
    lru = lru.reshape(LAYERS, 2, 2, CT, 2, 64, 64).transpose(0, 1, 4, 5, 2, 3, 6).reshape(LAYERS, 2, 2, 64, 2 * CT, 64)
    tokens = np.concatenate([x[0], ctx[0]], axis=0)
    return {
        "small": packed, "w_blocks": np.stack(blocks), "w_ada": w_ada,
        "pw": pw_w.reshape(LAYERS, CT, P, CT, P).transpose(0, 2, 3, 1, 4).reshape(LAYERS, P, CT * CT * P),
        "lru_w": lru, "xT": tokens.T.reshape(DT, P, TOK).transpose(1, 0, 2),
    }


def kernel(**inputs):
    import concourse.bacc as bacc
    from concourse.bass_utils import run_bass_kernel_spmd

    arrays = {n: np.ascontiguousarray(a) for n, a in _lay_out(**{n: np.asarray(a) for n, a in inputs.items()}).items()}

    def build(known):
        nc = bacc.Bacc("TRN2", target_bir_lowering=False, num_devices=1, dynamic_dma_scratch_size=64)
        io = {n: nc.dram_tensor("in_" + n, a.shape, mybir.dt.from_np(a.dtype), kind="ExternalInput").ap()
              for n, a in arrays.items()}
        io["out"] = nc.dram_tensor("out", (P, DT, LAT), F32, kind="ExternalOutput").ap()
        return nc, program(nc, io, known)

    marks = build({})[1]
    nc = build(marks)[0]
    r = run_bass_kernel_spmd(nc, [{"in_" + n: a for n, a in arrays.items()}], core_ids=[0])
    return r.results[0]["out"].transpose(1, 0, 2).reshape(D, LAT).T.reshape(1, LAT, D)
```

```python
from contextlib import ExitStack

import numpy as np
import concourse.bass as bass
from concourse import mybir

F32 = mybir.dt.float32
F32R = mybir.dt.float32r
ACT = mybir.ActivationFunctionType
ALU = mybir.AluOpType
AX = mybir.AxisListType

P = 128
D = 2048
DT = D // P
LAT, CTX = 256, 256
TOK = LAT + CTX
LAYERS = 2
HD = 128
HEADS, KV_HEADS, GROUP = 8, 2, 4
SCALE = HD ** -0.5
QB = 128
TAPS = 31
PAD = TAPS // 2
LTAPS = 4
CT = 4
EPS = 1e-6
ADA_KINDS = 3
SHIFT, SCL, GATE = range(3)
MASKED = -1e30

BLOCKS = ([("x", t) for t in range(CT)] + [("k", i) for i in range(KV_HEADS)] + [("v", i) for i in range(KV_HEADS)]
          + [(s, t) for t in range(CT) for s in ("b", "a")]
          + [("q", h) for h in range(4)] + [("ag", h) for h in range(4)]
          + [("q", h) for h in range(4, 8)] + [("ag", h) for h in range(4, 8)]
          + [("lg", t) for t in range(CT)] + [("cg", t) for t in range(CT)]
          + [("out", m) for m in range(DT)])
NB = len(BLOCKS)
B_OUT = NB - DT
COLUMN = {"x": 0, "k": 512, "v": 768, "a": 1024, "b": 1536, "cg": 2048, "lg": 2560, "q": 3072, "ag": 4096}
BOTH = 8

OPEN = [6, 4]
QT = DT // 4
HALF = DT // 2 * P

LRU_AT = [[6, 8, 11, 13], [4, 6, 9, 12]]
CONV_AT, CONV_STEPS = 12, 10
LN_AT = 32
PW_AT = 35
TP_LAG = [1, 2]
ROPE_AT = [{6: 4, 9: 5, 17: 16, 18: 17, 19: 18, 20: 19, 25: 24, 26: 25, 27: 26, 28: 27},
           {5: 4, 6: 5, 17: 16, 18: 17, 19: 18, 20: 19, 25: 24, 26: 25, 27: 26, 28: 27}]


def groups(l):
    if l == 0:
        out, s = {}, 22
        for kv in range(KV_HEADS):
            for ctx in (False, True):
                for qb in range(2):
                    out[s] = (kv, qb, ctx)
                    s += 2
        return out
    return {22: (0, 0, False), 25: (0, 1, False), 30: (1, 0, False), 33: (1, 1, False)}


def out_steps():
    return range(B_OUT, NB)


SMALL = [("c", DT * 2), ("ident", P), ("ones", P), ("perm", P), ("cos", LAT), ("sin", LAT), ("mask", 2 * P),
         ("norm_g", LAYERS * DT), ("final_g", DT), ("b_ada", LAYERS * ADA_KINDS * DT), ("dw_w", LAYERS * CT * TAPS),
         ("dw_b", LAYERS * CT), ("ln_g", LAYERS * CT), ("ln_b", LAYERS * CT), ("pw_b", LAYERS * CT),
         ("lcw", LAYERS * 2 * CT * LTAPS), ("lcb", LAYERS * 2 * CT), ("b_r", LAYERS * 2 * CT),
         ("b_i", LAYERS * 2 * CT), ("lam", LAYERS * 2 * CT), ("sink", LAYERS * HEADS)]
N_SMALL = sum(n for _, n in SMALL)


def ada_plan():
    rest = [(0, GATE, k) for k in range(DT)] + [(1, kind, k) for kind in (SHIFT, SCL, GATE) for k in range(DT)]
    steps = NB - OPEN[0]
    plan = {b: [rest.pop(0) for _ in range(2 if b < OPEN[0] + 4 * DT - steps else 1)] for b in range(OPEN[0], NB)}
    assert not rest
    return plan


def opening(l, quarter):
    return [("open", l, quarter, b, min(4, OPEN[l] - b)) for b in range(0, OPEN[l], 4)]


def unit(l, b, j):
    return 2 * (l * NB + b) + j


def open_unit(l, quarter, pair):
    return unit(l, 0, 0) + quarter * (OPEN[l] // 2) + pair


def stream():
    plan = ada_plan()
    s = []
    for quarter in range(4):
        s += [("ada0", kind, quarter, g) for kind in (SCL, SHIFT) for g in range(4)] + opening(0, quarter)
    s += [("w", b) for b in (OPEN[0], OPEN[0] + 1)]
    for l in range(LAYERS):
        for b in range(OPEN[l], NB):
            if b == PW_AT:
                s.append(("pw", l))
            if b + 2 < NB:
                s.append(("w", l * NB + b + 2))
            elif b + 2 == NB and l + 1 < LAYERS:
                s += opening(l + 1, 0)
            elif l + 1 < LAYERS:
                s += opening(l + 1, 1)
            if l == 0:
                s += [("ada", *a) for a in plan[b]]
        if l + 1 < LAYERS:
            s += opening(l + 1, 2) + opening(l + 1, 3)
            s += [("w", (l + 1) * NB + b) for b in (OPEN[l + 1], OPEN[l + 1] + 1)]
    return s


class Counts:

    def __init__(self, nc, ctx, known):
        self.nc, self.ctx, self.known = nc, ctx, known
        self.sems, self.n, self.marks = {}, {}, {}

    def sem(self, name):
        if name not in self.sems:
            self.sems[name] = self.ctx.enter_context(self.nc.semaphore(name))
            self.n[name] = 0
        return self.sems[name]

    def up(self, name, *key, by=1):
        s = self.sem(name)
        self.n[name] += by
        self.marks[(name, *key)] = self.n[name]
        return s, by

    def at(self, name, *key):
        return self.sem(name), self.known[(name, *key)] if self.known else 1

    def ago(self, name, n=0):
        return self.sem(name), self.n[name] - n


def program(nc, io, known):
    ctx = ExitStack()
    with ctx:
        def sb(name, shape, dt=F32):
            return ctx.enter_context(nc.sbuf_tensor(name, shape, dt))

        def pb(name, shape):
            return ctx.enter_context(nc.psum_tensor(name, shape, F32))

        NRAW = 3
        hh = sb("h_hi", [P, DT, TOK], F32R)
        hl = sb("h_lo", [P, DT, TOK], F32R)
        Y = sb("Y", [P, DT, TOK])
        raw = sb("raw", [P, NRAW, DT * P])
        wh = sb("w_hi", [P, 4, DT // 2 * P], F32R)
        wl = sb("w_lo", [P, 4, DT // 2 * P], F32R)
        T = sb("T", [P, 8, TOK])
        glu = sb("glu", [P, CT, 2, PAD + LAT + PAD])
        qreg = sb("qreg", [P, HEADS * TOK])
        kT = sb("kT", [P, KV_HEADS, TOK])
        v = sb("v", [P, 4, KV_HEADS * HD])
        bd = sb("bd", [P, 2, 2 * CT, P])
        tbuf = sb("tbuf", [P, TOK])
        lnr = sb("lnr", [P, TOK])
        cstat = sb("cstat", [P, DT, 32])
        adasb = lnr
        small = sb("small", [P, N_SMALL])
        der = sb("der", [P, LAYERS * (2 * 2 * CT + 2 * CT + HEADS)])
        ada = sb("ada", [P, LAYERS, 2, ADA_KINDS * DT])
        A = sb("A", [P, LAYERS, 2, DT])
        st = sb("stats", [P, 6, 4])
        eps = sb("eps", [P, 1])
        tiny = sb("tiny", [P, 3, 32])

        pB = [pb(f"psum_block{i}", [P, TOK]) for i in range(2)]
        psA = pb("psum_ada", [P, TOK])
        psM = pb("psum_misc", [P, TOK])
        psS = pb("psum_scores", [P, 4, TOK])

        q = qreg[:, :].rearrange("p (h t) -> p h t", h=HEADS)
        LW = LTAPS - 1 + LAT + LTAPS - 1
        lrux = qreg[:, HEADS * TOK - CT * 2 * LW:].rearrange("p (t s w) -> p t s w", t=CT, s=2)

        at = {}
        o = 0
        for name, n in SMALL:
            at[name] = small[:, o:o + n]
            o += n
        cT = at["c"].rearrange("p (k v) -> p k v", v=2)
        ident, ones, perm = at["ident"], at["ones"], at["perm"]
        cos, sin = at["cos"], at["sin"]
        mask = at["mask"].rearrange("p (m k) -> p m k", m=2)
        norm_g = at["norm_g"].rearrange("p (l k) -> p l k", l=LAYERS)
        b_ada = at["b_ada"].rearrange("p (l k) -> p l k", l=LAYERS)
        lcw = at["lcw"].rearrange("p (n k) -> p n k", k=LTAPS)
        sink = at["sink"]

        d0 = [0]

        def cut(n):
            d0[0] += n
            return der[:, d0[0] - n:d0[0]]

        dwh = at["dw_w"]
        hbr, hbi = at["b_r"], at["b_i"]
        s4n, s4 = cut(LAYERS * 2 * CT), cut(LAYERS * 2 * CT)
        lnhg, lnhb = cut(LAYERS * CT), cut(LAYERS * CT)
        nsink = cut(LAYERS * HEADS)

        C = Counts(nc, ctx, known)
        STREAM = stream()
        where = {s: i for i, s in enumerate(STREAM)}
        PLAN = ada_plan()
        GLOB = LAYERS * NB

        def arrived(item):
            i = where[item]
            return C.sem(f"raw{i % NRAW}"), 16 * (i // NRAW + 1)

        def raw_of(item):
            return raw[:, where[item] % NRAW, :]

        def source(u):
            l, r = divmod(u, 2 * NB)
            if r < 2 * OPEN[l]:
                quarter, pair = divmod(r, OPEN[l] // 2)
                return opening(l, quarter)[pair // 2], pair % 2
            return ("w", l * NB + r // 2), r % 2

        def block_done(gb):
            l, b = divmod(gb, NB)
            return C.at("mm", open_unit(l, 3, b // 2) if b < OPEN[l] else 2 * gb + 1)

        def bank(gb):
            l, b = divmod(gb, NB)
            return psS[:, b - 2, :] if 2 <= b < OPEN[l] else pB[gb % 2][:, :]

        def width(l, b):
            return TOK if l == 0 or b < BOTH else LAT

        def Yv(l, m):
            return Y[:, m, :] if l == 0 else Y[:, m, LAT:TOK]

        def segs(ap):
            return ap.rearrange("p (s t) -> p s t", t=LAT)

        def glu_in(l, t):
            return glu[:, t, 0:(2 if l == 0 else 1), PAD:PAD + LAT]

        def released(gb):
            kind = BLOCKS[gb % NB][0]
            return C.at("evac_act" if kind in "xkvbq" else "evac_dve", gb)

        def pw_bank(l, m):
            return psM if m % 2 == 0 else pB[(l * NB + PW_AT + 1) % 2]

        def conv_taps(b):
            j = b - CONV_AT
            if not 0 <= j < 2 * CONV_STEPS:
                return []
            pair, j = divmod(j, CONV_STEPS)
            lo, hi = TAPS * j // CONV_STEPS, TAPS * (j + 1) // CONV_STEPS
            return [(2 * pair + i, k) for k in range(lo, hi) for i in range(2)]

        block = ctx.enter_context(nc.Block())

        @block.sync
        def _(sp):
            sp.dma_start(small[:, :], io["small"]).then_inc(*C.up("small_in", by=16))

            def gate_weights(l):
                if l:
                    sp.wait_ge(*C.at("lru_mm", l - 1, CT - 1))
                else:
                    sp.wait_ge(*C.at("bd_zero"))
                for g in range(2):
                    for j in range(2):
                        sp.dma_start(bd[64 * j:64 * j + 64, g, :, 64 * j:64 * j + 64],
                                     io["lru_w"][l, g, j]).then_inc(*C.up("bd_in", l, g, j, by=16))

            def residual(m):
                if m < 2:
                    sp.wait_ge(*C.at("att_out", 0, max(groups(0))))
                else:
                    sp.wait_ge(*C.at("evac_dve", B_OUT + m - 2))
                sp.dma_start(T[:, m % 2, :], io["xT"][:, m, :]).then_inc(*C.up(f"xs{m % 2}", m, by=16))

            for i, item in enumerate(STREAM):
                if i >= NRAW:
                    old = STREAM[i - NRAW]
                    if old[0] == "w":
                        sp.wait_ge(*C.at("lo", 2 * old[1] + 1))
                    elif old[0] == "open":
                        sp.wait_ge(*C.at("lo", open_unit(old[1], old[2], (old[3] + old[4]) // 2 - 1)))
                    elif old[0] == "ada0":
                        sp.wait_ge(*C.at("ada0_mm", *old[1:]))
                    elif old[0] == "ada":
                        sp.wait_ge(*C.at("ada_mm", *old[1:]))
                    else:
                        sp.wait_ge(*C.at("pw_mm", old[1], CT - 1))
                dst = raw[:, i % NRAW, :]
                if item[0] == "w":
                    src = io["w_blocks"][item[1]]
                elif item[0] == "open":
                    l, quarter, b, n = item[1:]
                    src = io["w_blocks"][l * NB + b:l * NB + b + n, :, quarter * QT * P:(quarter + 1) * QT * P
                                         ].rearrange("b p c -> p b c")
                    dst = dst[:, 0:n * QT * P].rearrange("p (b c) -> p b c", b=n)
                elif item[0] == "ada0":
                    kind, quarter, g = item[1:]
                    at = kind * D + quarter * QT * P
                    src = io["w_ada"][0, g * QT * P:(g + 1) * QT * P, at:at + QT * P].rearrange("(j p) c -> p j c", p=P)
                    dst = dst.rearrange("p (j c) -> p j c", j=QT)
                elif item[0] == "pw":
                    src = io["pw"][item[1]]
                else:
                    l, kind, k = item[1:]
                    src = io["w_ada"][l, k * P:(k + 1) * P, kind * D:(kind + 1) * D]
                sp.dma_start(dst, src).then_inc(C.sem(f"raw{i % NRAW}"), 16)
                if i == NRAW - 1:
                    for g in range(4):
                        sp.dma_start(Y[:, 4 * g:4 * g + 4, :], io["xT"][:, 4 * g:4 * g + 4, :]).then_inc(*C.up(f"x_in{g}", by=16))
                if i == 2 * DT:
                    gate_weights(0)
                if item == ("w", B_OUT):
                    gate_weights(1)
                if item[0] == "w" and 0 <= item[1] - B_OUT - 2 < DT - 2:
                    residual(item[1] - B_OUT - 2)
                elif item[:2] == ("open", 1) and item[2] < 2:
                    residual(DT - 2 + item[2])
            for m in range(0, DT, 4):
                sp.wait_ge(*C.at("final", m + 3))
                sp.dma_start(io["out"][:, m:m + 4, :], Y[:, m:m + 4, 0:LAT]).then_inc(*C.up("stored", by=16))
            sp.wait_ge(*C.ago("stored"))

        @block.gpsimd
        def _(pool):
            nc.gpsimd.memset(cstat[:, :, :], 0.0).then_inc(*C.up("cstat_zero"))
            nc.gpsimd.memset(eps[:, :], EPS).then_inc(*C.up("eps_set"))
            nc.gpsimd.memset(bd[:, :, :, :], 0.0).then_inc(*C.up("bd_zero"))
            nc.gpsimd.memset(glu[:, :, :, :], 0.0).then_inc(*C.up("glu_zero"))
            for l in range(LAYERS):
                if l:
                    pool.wait_ge(*C.at("scores", l - 1, max(groups(l - 1))))
                nc.gpsimd.memset(lrux[:, :, :, :], 0.0).then_inc(*C.up("lrux_zero", l))

        @block.tensor
        def _(pe):
            mm = nc.tensor.matmul

            def ada_mm(l, kind, k):
                pe.wait_ge(*arrived(("ada", l, kind, k)))
                w = raw_of(("ada", l, kind, k))
                if k == 0:
                    pe.wait_ge(*(C.at("ada_out", *before(l, kind)) if (l, kind) != (0, GATE) else C.at("ada0_sum", SCL, 3)))
                for j in range(4):
                    last = mm(psA[32 * j:32 * j + 32, :], cstat[:, k, :], w[:, j * TOK:(j + 1) * TOK],
                              start=(k == 0), stop=(k == DT - 1), tile_position=(0, 32 * j))
                last.then_inc(*C.up("ada_mm", l, kind, k))

            def ada_tp(l, kind):
                pe.wait_ge(*C.at("ada_rows", l, kind))
                for j in range(4):
                    last = nc.tensor.transpose(psA[:, j * P:(j + 1) * P], adasb[:, j * P:(j + 1) * P], ident)
                last.then_inc(*C.up("ada_tp", l, kind))

            def ada0_mm(kind, quarter, g):
                pe.wait_ge(*arrived(("ada0", kind, quarter, g)))
                w = raw_of(("ada0", kind, quarter, g))
                ps = psA if kind == SCL else psM
                if g == 0 and quarter:
                    pe.wait_ge(*C.at("ada0_sum", kind, quarter - 1))
                for j in range(4):
                    last = mm(ps[32 * j:32 * j + 32, :], cstat[:, g * QT + j, :], w[:, j * TOK:(j + 1) * TOK],
                              start=(g == 0), stop=(g == 3), tile_position=(0, 32 * j))
                last.then_inc(*C.up("ada0_mm", kind, quarter, g))

            def ada0_tp(kind, quarter):
                pe.wait_ge(*C.at("ada0_rows", kind, quarter))
                ps = psA if kind == SCL else psM
                for j in range(4):
                    last = nc.tensor.transpose(ps[:, j * P:(j + 1) * P], T[:, 6 + kind, j * P:(j + 1) * P], ident)
                last.then_inc(*C.up("ada0_tp", kind, quarter))

            def rms_mm(l):
                n = TOK if l < LAYERS else LAT
                pe.wait_ge(*C.at("rms_add", l, DT - 1))
                mm(psS[:, 0, 0:n], ones, T[:, 4, 0:n], start=True, stop=True).then_inc(*C.up("rms_mm", l))

            def mm_open(l, quarter, pair, aside=()):
                u = open_unit(l, quarter, pair)
                pe.wait_ge(*C.at("lo", u))
                for b in (2 * pair, 2 * pair + 1):
                    if quarter == 0:
                        if l and b < 2:
                            pe.wait_ge(*released(l * NB + b - 2))
                        elif b == 2:
                            pe.wait_ge(*C.at("rms_std", l))
                aside = list(aside)
                for i in range(QT):
                    k = quarter * QT + i
                    if pair == 0:
                        pe.wait_ge(*C.at("h_lo", l, k))
                    for c, b in enumerate((2 * pair, 2 * pair + 1)):
                        ps = bank(l * NB + b)
                        at = (c * QT + i) * P
                        hi, lo = wh[:, u % 4, at:at + P], wl[:, u % 4, at:at + P]
                        mm(ps, hi, hh[:, k, :], start=(k == 0), stop=False)
                        mm(ps, hi, hl[:, k, :], start=False, stop=False)
                        last = mm(ps, lo, hh[:, k, :], start=False, stop=(k == DT - 1))
                    if i == QT - 1:
                        last.then_inc(*C.up("mm", u))
                    if aside:
                        ada0_mm(*aside.pop(0))

            def mm_half(gb, j):
                l, b = divmod(gb, NB)
                n = width(l, b)
                ps = pB[gb % 2]
                pe.wait_ge(*C.at("lo", 2 * gb + j))
                if j == 0 and b == PW_AT + 1:
                    pe.wait_ge(*C.at("pw_out", l, CT - 1))
                elif j == 0 and gb >= 2:
                    pe.wait_ge(*released(gb - 2))
                slot = (2 * gb + j) % 4
                for i in range(DT // 2):
                    k = j * DT // 2 + i
                    if b == B_OUT:
                        pe.wait_ge(*C.at("y_lo", l, k))
                    hi, lo = wh[:, slot, i * P:(i + 1) * P], wl[:, slot, i * P:(i + 1) * P]
                    mm(ps[:, 0:n], hi, hh[:, k, 0:n], start=(k == 0), stop=False)
                    mm(ps[:, 0:n], hi, hl[:, k, 0:n], start=False, stop=False)
                    last = mm(ps[:, 0:n], lo, hh[:, k, 0:n], start=False, stop=(k == DT - 1))
                last.then_inc(*C.up("mm", 2 * gb + j))

            def rope_mm(l, b):
                kind, i = BLOCKS[b]
                if not misc:
                    pe.wait_ge(*C.at("ada0_sum", SHIFT, 3))
                pe.wait_ge(*C.at("evac_act", l * NB + b))
                misc_free(l)
                src = kT[:, i, 0:LAT] if kind == "k" else q[:, i, 0:LAT]
                mm(psM[:, 0:LAT], perm, src, start=True, stop=True).then_inc(*C.up("rope_mm", l, kind, i))

            def misc_free(l):
                if misc:
                    pe.wait_ge(*C.at(*misc[-1]))

            misc = []
            scores_free = []

            def lru_mm(l, t):
                pe.wait_ge(*C.at("taps", l, t, 1))
                if t == 0:
                    pe.wait_ge(*C.at("bd_in", l, 1, 1))
                    for b in range(2, OPEN[l]):
                        pe.wait_ge(*C.at("evac_act", l * NB + b))
                else:
                    pe.wait_ge(*C.at("lru_tanh", l, t - 1, 1))
                for d in range(2):
                    for g in range(2):
                        last = mm(psS[:, 2 * d + g, :], bd[:, g, d * CT + t, :], T[:, 4 * d, :], start=True, stop=True)
                last.then_inc(*C.up("lru_mm", l, t))

            def scores(l, s):
                kv, qb, isctx = groups(l)[s]
                pe.wait_ge(*C.at("rope", l, "k", KV_HEADS - 1))
                if isctx:
                    pe.wait_ge(*C.at("evac_act", l * NB + 16 + 8 * kv + 3))
                else:
                    pe.wait_ge(*C.at("rope", l, "q", GROUP * kv + GROUP - 1))
                if scores_free:
                    pe.wait_ge(*C.at("att_out", l, scores_free[-1]))
                else:
                    pe.wait_ge(*C.at("lru_tanh", l, CT - 1, 1))
                t0 = (LAT if isctx else 0) + qb * QB
                for g in range(GROUP):
                    qt = q[:, GROUP * kv + g, t0:t0 + QB]
                    if isctx:
                        last = mm(psS[:, g, LAT:TOK], qt, kT[:, kv, LAT:TOK], start=True, stop=True)
                    else:
                        mm(psS[:, g, :], qt, kT[:, kv, :], start=True, stop=False)
                        far = (1 - qb) * QB
                        last = mm(psS[:, g, far:far + QB], ident, mask[:, qb, :], start=False, stop=True)
                last.then_inc(*C.up("scores", l, s))
                scores_free.append(s)

            def p_tp(l, s):
                isctx = groups(l)[s][2]
                for g in range(GROUP):
                    pe.wait_ge(*C.at("probs", l, s, g))
                    for kt in range(2 if isctx else 0, 4):
                        last = nc.tensor.transpose(psS[:, g, kt * P:(kt + 1) * P], T[:, g, kt * P:(kt + 1) * P], ident)
                    last.then_inc(*C.up("p_tp", l, s, g))

            def pv(l, s):
                kv, qb, isctx = groups(l)[s]
                pe.wait_ge(*C.at("pT", l, s, GROUP - 1))
                pe.wait_ge(*C.at("v_out", l, KV_HEADS - 1))
                first = 2 if isctx else 0
                for kt in range(first, 4):
                    last = mm(psS[:, 0, :], v[:, kt, kv * HD:(kv + 1) * HD], T[:, 4 + kt, :],
                              start=(kt == first), stop=(kt == 3))
                last.then_inc(*C.up("pv", l, s))

            def ln_mm(l, stage):
                n = TOK if l == 0 else LAT
                misc_free(l)
                if stage == "ln_sum":
                    for t in range(CT):
                        pe.wait_ge(*C.at("conv", l, t, TAPS - 1))
                        last = mm(psM[:, 0:n], ones, Yv(l, t), start=(t == 0), stop=(t == CT - 1))
                    misc.append(("ln_c", l, CT - 1))
                else:
                    for t in range(CT):
                        pe.wait_ge(*C.at("ln_sq", l, t))
                        last = mm(psM[:, 0:n] if l else segs(psM[:, 0:n]), ones, glu_in(l, t) if l == 0 else glu[:, t, 0, PAD:PAD + LAT],
                                  start=(t == 0), stop=(t == CT - 1))
                    misc.append(("ln_std", l))
                last.then_inc(*C.up(stage, l))

            def pw_mm(l, m):
                n = TOK if l == 0 else LAT
                if m < 2:
                    misc_free(l)
                    pe.wait_ge(*released(l * NB + PW_AT - 1))
                else:
                    pe.wait_ge(*C.at("pw_out", l, m - 2))
                if m == 0:
                    pe.wait_ge(*arrived(("pw", l)))
                w = raw_of(("pw", l)).rearrange("p (m k c) -> p m k c", m=CT, k=CT)
                for k in range(CT):
                    if m == 0:
                        pe.wait_ge(*C.at("ln_y", l, k))
                    last = mm(pw_bank(l, m)[:, 0:n], w[:, m, k, :], Yv(l, k), start=(k == 0), stop=(k == CT - 1))
                last.then_inc(*C.up("pw_mm", l, m))

            order = [(0, GATE), (1, SHIFT), (1, SCL), (1, GATE)]

            def before(l, kind):
                return order[order.index((l, kind)) - 1]

            pe.wait_ge(*C.at("small_in"))
            pe.wait_ge(*C.at("cstat", 1))
            for kind in (SCL, SHIFT):
                for g in range(4):
                    ada0_mm(kind, 0, g)
            rms_mm(0)
            ada0_tp(SCL, 0)
            ada0_tp(SHIFT, 0)

            for gb in range(GLOB):
                l, b = divmod(gb, NB)
                if b == 0:
                    scores_free.clear()
                    if l:
                        rms_mm(l)
                    for quarter in range(4):
                        nxt = [(kind, quarter + 1, g) for kind in (SCL, SHIFT) for g in range(4)] if l == 0 and quarter < 3 else []
                        for pair in range(OPEN[l] // 2):
                            mm_open(l, quarter, pair, nxt[3 * pair:3 * pair + 3])
                        if nxt:
                            ada0_tp(SCL, quarter + 1)
                            ada0_tp(SHIFT, quarter + 1)
                    if l:
                        for a in PLAN[NB - 1]:
                            if a[2] == DT - 1:
                                ada_tp(*a[:2])
                if b < OPEN[l]:
                    continue
                mm_half(gb, 0)
                for a in (PLAN[b - 1] if l == 0 and b - 1 in PLAN else []):
                    if a[2] == DT - 1:
                        ada_tp(*a[:2])
                if b - TP_LAG[l] - 1 in groups(l):
                    pv(l, b - TP_LAG[l] - 1)
                mm_half(gb, 1)
                if b in ROPE_AT[l]:
                    rope_mm(l, ROPE_AT[l][b])
                    misc.append(("rope_t", l, *BLOCKS[ROPE_AT[l][b]]))
                if b and BLOCKS[b - 1][0] == "v":
                    i = BLOCKS[b - 1][1]
                    pe.wait_ge(*C.at("evac_act", gb - 1))
                    misc_free(l)
                    for kt in range(4):
                        last = nc.tensor.transpose(psM[:, kt * P:(kt + 1) * P], tbuf[:, kt * P:(kt + 1) * P], ident)
                    last.then_inc(*C.up("v_tp", l, i))
                    misc.append(("v_out", l, i))
                if b - 1 in LRU_AT[l]:
                    lru_mm(l, LRU_AT[l].index(b - 1))
                if b in groups(l):
                    scores(l, b)
                if b - TP_LAG[l] in groups(l):
                    p_tp(l, b - TP_LAG[l])
                if b == LN_AT:
                    ln_mm(l, "ln_sum")
                if b == LN_AT + 1:
                    ln_mm(l, "ln_var")
                if b == PW_AT:
                    for m in range(CT):
                        pw_mm(l, m)
                    misc.append(("pw_out", l, CT - 1))
                if l == 0:
                    for a in PLAN[b]:
                        ada_mm(*a)
            rms_mm(LAYERS)

        @block.scalar
        def _(act):
            fn = nc.scalar.activation

            def hi(u):
                item, j = source(u)
                act.wait_ge(*arrived(item))
                if u >= 4:
                    act.wait_ge(*C.at("mm", u - 4))
                fn(wh[:, u % 4, :], raw_of(item)[:, j * HALF:(j + 1) * HALF], ACT.Copy).then_inc(*C.up("hi", u))

            def ada_rows(l, kind):
                act.wait_ge(*C.at("ada_mm", l, kind, DT - 1))
                act.wait_ge(*C.at(*{(0, GATE): ("rope", 0, "k", 1), (1, SHIFT): ("rope", 0, "q", 3),
                                    (1, SCL): ("ln_n", 0, CT - 1), (1, GATE): ("ln_n", 0, CT - 1)}[l, kind]))
                fn(adasb[:, :], psA[:, :], ACT.Copy).then_inc(*C.up("ada_rows", l, kind))

            def ada0_rows(quarter):
                for kind in (SCL, SHIFT):
                    act.wait_ge(*C.at("ada0_mm", kind, quarter, 3))
                    fn(T[:, 6 + kind, :], (psA if kind == SCL else psM)[:, :], ACT.Copy).then_inc(*C.up("ada0_rows", kind, quarter))

            def square(l, m):
                n = TOK if l < LAYERS else LAT
                if l == 0:
                    act.wait_ge(*C.at(f"x_in{m // 4}"))
                else:
                    act.wait_ge(*C.at("evac_dve", (l - 1) * NB + B_OUT + m))
                if m >= 3:
                    act.wait_ge(*C.at("rms_add", l, m - 2))
                elif l:
                    act.wait_ge(*C.at("att_out", l - 1, max(groups(l - 1))))
                dst = T[:, 4 if m == 0 else 2 + m % 2, 0:n]
                fn(dst, Y[:, m, 0:n], ACT.Square).then_inc(*C.up("rms_sq", l, m))

            def rms_std(l):
                n = TOK if l < LAYERS else LAT
                act.wait_ge(*C.at("rms_mm", l))
                fn(tbuf[:, 0:n], psS[:, 0, 0:n], ACT.Sqrt, scale=1.0 / D, bias=eps[:, 0:1]).then_inc(*C.up("rms_std", l))

            def modulate(l, k):
                act.wait_ge(*C.at("mod", l, k, 1))
                for i in range(2):
                    fn(hh[:, k, i * LAT:(i + 1) * LAT], T[:, k % 2, i * LAT:(i + 1) * LAT], ACT.Identity,
                       bias=ada[:, l, i, SHIFT * DT + k:SHIFT * DT + k + 1]).then_inc(*C.up("h_hi", l, k, i))

            def evac(gb):
                l, b = divmod(gb, NB)
                kind, i = BLOCKS[b]
                n = width(l, b)
                if kind == "out":
                    return
                ps = bank(gb)[:, 0:n]
                act.wait_ge(*block_done(gb))
                if kind == "x":
                    act.wait_ge(*C.at("lrux_zero", l))
                    fn(lrux[:, i, :, LTAPS - 1:LTAPS - 1 + LAT], segs(ps), ACT.Copy).then_inc(*C.up("evac_act", gb))
                elif kind == "k":
                    fn(kT[:, i, :], ps, ACT.Copy).then_inc(*C.up("evac_act", gb))
                elif kind == "v":
                    if i:
                        act.wait_ge(*C.at("v_tp", l, i - 1))
                    fn(tbuf[:, :], ps, ACT.Copy).then_inc(*C.up("evac_act", gb))
                elif kind == "b":
                    if i == 0:
                        act.wait_ge(*C.at("v_tp", l, KV_HEADS - 1))
                    else:
                        act.wait_ge(*C.at("evac_dve", gb - 1))
                    fn(tbuf[:, 0:n], ps, ACT.Tanh, scale=0.5).then_inc(*C.up("evac_act", gb))
                elif kind == "q":
                    if i == 0:
                        act.wait_ge(*C.at("lru_h", l, CT - 1))
                    fn(q[:, i, 0:n], ps, ACT.Copy).then_inc(*C.up("evac_act", gb))
                elif kind == "ag":
                    fn(Yv(l, 8 + i), ps, ACT.Tanh, scale=0.5).then_inc(*C.up("gate_tanh", gb))
                elif kind in ("lg", "cg"):
                    if (kind, i) != ("lg", 0):
                        act.wait_ge(*C.at("evac_dve", gb - 1))
                    fn(tbuf[:, 0:n], ps, ACT.Tanh, scale=0.5).then_inc(*C.up("gate_tanh", gb))

            def lru_act(l, t):
                act.wait_ge(*C.at("lru_mm", l, t))
                for d in range(2):
                    c = (l * 2 + d) * CT + t
                    fn(T[:, 4 * d + 1, :], psS[:, 2 * d, :], ACT.Tanh, scale=0.5, bias=hbr[:, c:c + 1]
                       ).then_inc(*C.up("lru_tanh", l, t, d, "r"))
                    fn(T[:, 4 * d + 2, :], psS[:, 2 * d + 1, :], ACT.Tanh, scale=0.5, bias=hbi[:, c:c + 1]
                       ).then_inc(*C.up("lru_tanh", l, t, d))
                for d in range(2):
                    c = (l * 2 + d) * CT + t
                    act.wait_ge(*C.ago("lru_tanh", 2 - 2 * d + 1))
                    fn(T[:, 4 * d + 3, :], T[:, 4 * d + 1, :], ACT.Exp, scale=s4n[:, c:c + 1], bias=s4n[:, c:c + 1]
                       ).then_inc(*C.up("lru_a", l, t, d))
                for d in range(2):
                    c = (l * 2 + d) * CT + t
                    act.wait_ge(*C.ago("lru_a", 1 - d))
                    fn(T[:, 4 * d + 1, :], T[:, 4 * d + 1, :], ACT.Tanh, scale=s4[:, c:c + 1], bias=s4[:, c:c + 1]
                       ).then_inc(*C.up("lru_t", l, t, d))
                for d in range(2):
                    fn(q[:, d, :], T[:, 4 * d + 3, :], ACT.Square).then_inc(*C.up("lru_a2", l, t, d))

            def lru_sqrt(l, t):
                for d in range(2):
                    act.wait_ge(*C.at("lru_v", l, t, d))
                    fn(q[:, d, :], q[:, d, :], ACT.Sqrt, scale=0.25).then_inc(*C.up("lru_sq", l, t, d))

            def att_exp(l, s):
                kv, qb, isctx = groups(l)[s]
                k0 = LAT if isctx else 0
                act.wait_ge(*C.at("att_neg", l, s))
                if s != min(groups(l)):
                    act.wait_ge(*C.at("p_tp", l, max(x for x in groups(l) if x < s), GROUP - 1))
                for g in range(GROUP):
                    fn(T[:, g, k0:TOK], psS[:, g, k0:TOK], ACT.Exp, scale=SCALE, bias=st[:, 1, g:g + 1],
                       accum_out=st[:, 2, g:g + 1]).then_inc(*C.up("att_exp", l, s, g))
                act.wait_ge(*C.at("att_sn", l, s))
                fn(st[:, 4, :], st[:, 3, :], ACT.Exp).then_inc(*C.up("att_es", l, s))

            def att_pT(l, s):
                isctx = groups(l)[s][2]
                k0 = 2 if isctx else 0
                if s != min(groups(l)):
                    act.wait_ge(*C.at("pv", l, max(x for x in groups(l) if x < s)))
                for g in range(GROUP):
                    act.wait_ge(*C.at("p_tp", l, s, g))
                    fn(T[:, 4 + k0:8, g * QB:(g + 1) * QB],
                       psS[:, g, k0 * P:TOK].rearrange("p (k q) -> p k q", q=P), ACT.Copy).then_inc(*C.up("pT", l, s, g))

            act.wait_ge(*C.at("small_in"))
            fn(tiny[:, 0, :], at["c"], ACT.Tanh, scale=0.5).then_inc(*C.up("c_tanh"))
            n = LAYERS * 2 * CT
            fn(tiny[:, 1, 0:n], at["lam"], ACT.Abs).then_inc(*C.up("lam_abs"))
            act.wait_ge(*C.ago("lam_abs"))
            fn(tiny[:, 1, 0:n], tiny[:, 1, 0:n], ACT.Exp, scale=-1.0).then_inc(*C.up("lam_exp"))
            act.wait_ge(*C.at("lam_one"))
            fn(tiny[:, 2, 0:n], tiny[:, 1, 0:n], ACT.Ln).then_inc(*C.up("lam_ln"))
            act.wait_ge(*C.at("eps_set"))
            for k in range(DT):
                square(0, k)
            for gb in range(GLOB):
                l, b = divmod(gb, NB)
                if b == 0:
                    if l:
                        square(l, DT - 1)
                    rms_std(l)
                    u0, n = unit(l, 0, 0), OPEN[l] // 2
                    if l == 0:
                        for quarter in range(4):
                            ada0_rows(quarter)
                            for k in range(quarter * QT, (quarter + 1) * QT):
                                modulate(l, k)
                            for i in range(n):
                                hi(u0 + n * quarter + i)
                    else:
                        for quarter in range(4):
                            for k in range(quarter * QT, (quarter + 1) * QT):
                                modulate(l, k)
                            for i in range(n if 0 < quarter < 3 else 0):
                                hi(u0 + 4 + n * (quarter - 1) + i)
                    for i in range(4):
                        hi(u0 + 2 * OPEN[l] + i)
                        if i:
                            for c in range(2):
                                if 2 * (i - 1) + c < OPEN[l]:
                                    evac(gb + 2 * (i - 1) + c)
                if b < OPEN[l]:
                    continue
                if b == B_OUT:
                    for k in range(DT):
                        if k == 0:
                            act.wait_ge(*C.at("mm", 2 * gb - 1))
                            act.wait_ge(*C.at("att_out", l, max(groups(l))))
                            act.wait_ge(*C.at("evac_dve", gb - 1))
                        n = width(l, b)
                        fn(hh[:, k, 0:n], Yv(l, k), ACT.Copy).then_inc(*C.up("y_hi", l, k))
                if gb + 2 < GLOB:
                    hi(2 * gb + 4)
                    hi(2 * gb + 5)
                evac(gb)
                if b and BLOCKS[b - 1][0] == "v":
                    i = BLOCKS[b - 1][1]
                    act.wait_ge(*C.at("v_tp", l, i))
                    fn(v[:, :, i * HD:(i + 1) * HD], psM[:, :].rearrange("p (k d) -> p k d", d=HD), ACT.Copy
                       ).then_inc(*C.up("v_out", l, i))
                if b - 2 in LRU_AT[l]:
                    lru_sqrt(l, LRU_AT[l].index(b - 2))
                if b - 1 in LRU_AT[l]:
                    lru_act(l, LRU_AT[l].index(b - 1))
                if b - TP_LAG[l] in groups(l):
                    att_pT(l, b - TP_LAG[l])
                if b in groups(l):
                    att_exp(l, b)
                if b == LN_AT:
                    for t in range(CT):
                        act.wait_ge(*C.at("ln_c", l, t))
                        fn(glu_in(l, t), segs(Yv(l, t)), ACT.Square).then_inc(*C.up("ln_sq", l, t))
                if b == LN_AT + 1:
                    n = width(l, b)
                    act.wait_ge(*C.at("ln_var", l))
                    fn(lnr[:, 0:n], psM[:, 0:n], ACT.Sqrt, scale=1.0 / (CT * P), bias=eps[:, 0:1]
                       ).then_inc(*C.up("ln_std", l))
                if b == LN_AT + 2:
                    for t in range(CT):
                        c = l * CT + t
                        act.wait_ge(*C.at("ln_n", l, t))
                        fn(glu_in(l, t), segs(Yv(l, t)), ACT.Tanh, scale=lnhg[:, c:c + 1], bias=lnhb[:, c:c + 1]
                           ).then_inc(*C.up("ln_th", l, t))
                for m in range(CT if b == PW_AT else 0):
                    n = width(l, b)
                    c = l * CT + m
                    act.wait_ge(*C.at("pw_mm", l, m))
                    if m == 0:
                        act.wait_ge(*C.at("ln_y", l, CT - 1))
                    fn(glu_in(l, m), segs(pw_bank(l, m)[:, 0:n]), ACT.Identity, scale=0.5, bias=at["pw_b"][:, c:c + 1]
                       ).then_inc(*C.up("pw_out", l, m))
                if b - B_OUT >= 1:
                    square(l + 1, b - B_OUT - 1)
                if l == 0:
                    for a in PLAN[b]:
                        if a[2] == DT - 1:
                            ada_rows(*a[:2])
            square(LAYERS, DT - 1)
            rms_std(LAYERS)

        @block.vector
        def _(dve):
            V = nc.vector
            stt = V.scalar_tensor_tensor

            def lo(u):
                item, j = source(u)
                dve.wait_ge(*C.at("hi", u))
                V.tensor_tensor(wl[:, u % 4, :], raw_of(item)[:, j * HALF:(j + 1) * HALF], wh[:, u % 4, :].bitcast(F32),
                                ALU.subtract).then_inc(*C.up("lo", u))

            def ada0_out(quarter):
                for kind in (SCL, SHIFT):
                    dve.wait_ge(*C.at("ada0_tp", kind, quarter))
                    ps = (psA if kind == SCL else psM)[:, :].rearrange("p (q j r) -> p r q j", q=4, j=4)
                    V.tensor_reduce(tiny[:, 1 + kind, 0:8].rearrange("p (r q) -> p r q", r=2), ps[:, 0:2], axis=AX.X,
                                    op=ALU.add).then_inc(*C.up("ada0_sum", kind, quarter))
                dve.wait_ge(*C.ago("ada0_sum"))
                for kind in (SCL, SHIFT):
                    at = kind * DT + quarter * QT
                    for i in range(2):
                        V.tensor_tensor(ada[:, 0, i, at:at + QT], tiny[:, 1 + kind, 4 * i:4 * i + 4], b_ada[:, 0, at:at + QT],
                                        ALU.add).then_inc(*C.up("ada_out", 0, kind, quarter))
                q4 = slice(quarter * QT, (quarter + 1) * QT)
                dve.wait_ge(*C.ago("ada_out"))
                for i in range(2):
                    stt(A[:, 0, i, q4], ada[:, 0, i, SCL * DT + quarter * QT:SCL * DT + (quarter + 1) * QT], 1.0,
                        norm_g[:, 0, q4], ALU.add, ALU.mult).then_inc(*C.up("A", 0, i))
                dve.wait_ge(*C.ago("A"))

            def rms_add(l, m):
                n = TOK if l < LAYERS else LAT
                dve.wait_ge(*C.at("rms_sq", l, m))
                if m == 0:
                    return
                if m > 1:
                    dve.wait_ge(*C.ago("rms_add"))
                V.tensor_tensor(T[:, 4, 0:n], T[:, 4, 0:n], T[:, 2 + m % 2, 0:n], ALU.add
                                ).then_inc(*(C.up("rms_add", l, m)))

            def ada_out(l, kind):
                dve.wait_ge(*C.at("ada_tp", l, kind))
                cols = psA[:, :].rearrange("p (q j r) -> p q j r", q=4, j=4)
                for i in range(2):
                    V.tensor_tensor(ada[:, l, i, kind * DT:(kind + 1) * DT].rearrange("p (j q) -> p q j", q=4),
                                    cols[:, :, :, i], b_ada[:, l, kind * DT:(kind + 1) * DT].rearrange("p (j q) -> p q j", q=4),
                                    ALU.add).then_inc(*C.up("ada_out", l, kind))
                if kind == SCL:
                    for i in range(2):
                        dve.wait_ge(*C.ago("ada_out", 0))
                        stt(A[:, l, i, :], ada[:, l, i, SCL * DT:(SCL + 1) * DT], 1.0, norm_g[:, l, :], ALU.add, ALU.mult
                            ).then_inc(*C.up("A", l, i))

            def modulate(l, k):
                for i in range(2):
                    w = slice(i * LAT, (i + 1) * LAT)
                    stt(T[:, k % 2, w], Y[:, k, w], A[:, l, i, k:k + 1], tbuf[:, w], ALU.mult, ALU.mult
                        ).then_inc(*C.up("mod", l, k, i))

            def h_lo(l, k):
                for i in range(2):
                    w = slice(i * LAT, (i + 1) * LAT)
                    dve.wait_ge(*C.at("h_hi", l, k, i))
                    stt(hl[:, k, w], T[:, k % 2, w], ada[:, l, i, SHIFT * DT + k:SHIFT * DT + k + 1],
                        hh[:, k, w].bitcast(F32), ALU.add, ALU.subtract).then_inc(*C.up("h_lo", l, k))

            def rstd(l):
                n = TOK if l < LAYERS else LAT
                dve.wait_ge(*C.at("rms_std", l))
                V.reciprocal(tbuf[:, 0:n], tbuf[:, 0:n]).then_inc(*C.up("rstd", l))
                dve.wait_ge(*C.ago("rstd"))

            def h_quarter(l, quarter):
                for k in range(quarter * QT, (quarter + 1) * QT):
                    if l and k < 2:
                        dve.wait_ge(*C.ago("evac_dve"))
                    if k >= 2:
                        dve.wait_ge(*C.at("h_lo", l, k - 2))
                    modulate(l, k)
                    if k > quarter * QT:
                        h_lo(l, k - 1)
                h_lo(l, (quarter + 1) * QT - 1)

            def evac(gb):
                l, b = divmod(gb, NB)
                kind, i = BLOCKS[b]
                n = width(l, b)
                ps = bank(gb)[:, 0:n]
                if kind == "a":
                    dve.wait_ge(*C.at("mm", 2 * gb + 1))
                    dve.wait_ge(*C.at("evac_act", gb - 1))
                    dve.wait_ge(*C.at("glu_zero"))
                    stt(glu_in(l, i), segs(tbuf[:, 0:n]), 1.0, segs(ps), ALU.add, ALU.mult).then_inc(*C.up("evac_dve", gb))
                elif kind == "ag":
                    dve.wait_ge(*C.at("gate_tanh", gb))
                    stt(Yv(l, 8 + i), Yv(l, 8 + i), 1.0, ps, ALU.add, ALU.mult).then_inc(*C.up("evac_dve", gb))
                elif kind in ("lg", "cg"):
                    dve.wait_ge(*C.at("gate_tanh", gb))
                    stt(tbuf[:, 0:n], tbuf[:, 0:n], 1.0, ps, ALU.add, ALU.mult).then_inc(*C.up("gated", gb))
                    dve.wait_ge(*C.ago("gated"))
                    if kind == "lg":
                        stt(Yv(l, 4 + i), tbuf[:, 0:n], 0.5, Yv(l, 4 + i), ALU.mult, ALU.mult
                            ).then_inc(*C.up("evac_dve", gb))
                    else:
                        dve.wait_ge(*C.at("pw_out", l, i))
                        if i == 0:
                            dve.wait_ge(*C.at("pw_mm", l, CT - 1))
                        stt(segs(Yv(l, i)), segs(tbuf[:, 0:n]), 0.5, glu_in(l, i), ALU.mult, ALU.mult
                            ).then_inc(*C.up("evac_dve", gb))
                elif kind == "out":
                    dve.wait_ge(*C.at("mm", 2 * gb + 1))
                    if l == 0:
                        dve.wait_ge(*C.at(f"xs{i % 2}", i))
                    for s in range(n // LAT):
                        w = slice(s * LAT, (s + 1) * LAT)
                        old = T[:, i % 2, w] if l == 0 else Y[:, i, w]
                        stt(Y[:, i, w], ps[:, w], ada[:, l, s, GATE * DT + i:GATE * DT + i + 1], old, ALU.mult, ALU.add
                            ).then_inc(*C.up("evac_dve", gb))

            def rope(l, b):
                kind, i = BLOCKS[b]
                x = kT[:, i, 0:LAT] if kind == "k" else q[:, i, 0:LAT]
                dve.wait_ge(*C.at("rope_mm", l, kind, i))
                if (l, kind, i) != (0, "k", 0):
                    dve.wait_ge(*C.ago("rope"))
                V.tensor_tensor(lnr[:, 0:LAT], psM[:, 0:LAT], sin, ALU.mult).then_inc(*C.up("rope_t", l, kind, i))
                V.tensor_tensor(x, x, cos, ALU.mult).then_inc(*C.up("rope_c", l, kind, i))
                dve.wait_ge(*C.ago("rope_c"))
                V.tensor_tensor(x, x, lnr[:, 0:LAT], ALU.add).then_inc(*C.up("rope", l, kind, i))

            def taps(l, t):
                if t == 0:
                    dve.wait_ge(*C.ago("h_lo"))
                dve.wait_ge(*C.at("evac_act", l * NB + t))
                if t:
                    dve.wait_ge(*C.ago("lru_h"))
                for k in range(LTAPS):
                    for d in range(2):
                        c = (l * 2 + d) * CT + t
                        s = k if d == 0 else 2 * (LTAPS - 1) - k
                        x = lrux[:, t, :, s:s + LAT]
                        out = segs(T[:, 4 * d, :])
                        if k == 0:
                            V.tensor_scalar(out, x, lcw[:, c, 0:1], at["lcb"][:, c:c + 1], ALU.mult, ALU.add
                                            ).then_inc(*C.up("taps", l, t, d))
                        else:
                            dve.wait_ge(*C.ago("taps", 1))
                            stt(out, x, lcw[:, c, k:k + 1], out, ALU.mult, ALU.add).then_inc(*C.up("taps", l, t, d))

            def lru_v(l, t):
                for d in range(2):
                    dve.wait_ge(*C.at("lru_a2", l, t, d))
                    stt(q[:, d, :], q[:, d, :], 1.0, T[:, 4 * d + 1, :], ALU.add, ALU.mult).then_inc(*C.up("lru_v", l, t, d))
                for d in range(2):
                    stt(T[:, 4 * d + 2, :], T[:, 4 * d + 2, :], 1.0, T[:, 4 * d, :], ALU.add, ALU.mult
                        ).then_inc(*C.up("lru_g", l, t, d))

            def lru_scan(l, t):
                for d in range(2):
                    dve.wait_ge(*C.at("lru_sq", l, t, d))
                    dve.wait_ge(*C.ago("lru_g"))
                    V.tensor_tensor(T[:, 4 * d + 2, :], T[:, 4 * d + 2, :], q[:, d, :], ALU.mult
                                    ).then_inc(*C.up("lru_b", l, t, d))
                dve.wait_ge(*C.ago("lru_b", 1))
                f, r = T[:, 0, :], T[:, 4, :]
                V.tensor_tensor_scan(f[:, LAT:TOK], T[:, 3, LAT:TOK], T[:, 2, LAT:TOK], 0.0, ALU.mult, ALU.add
                                     ).then_inc(*C.up("lru_scan", l, t))
                dve.wait_ge(*C.ago("lru_b"))
                V.tensor_tensor_scan(r[:, ::-1], T[:, 7, ::-1], T[:, 6, ::-1], 0.0, ALU.mult, ALU.add
                                     ).then_inc(*C.up("lru_scan", l, t))
                dve.wait_ge(*C.ago("lru_scan", 1))
                V.tensor_tensor_scan(f[:, 0:LAT], T[:, 3, 0:LAT], T[:, 2, 0:LAT], f[:, TOK - 1:TOK], ALU.mult, ALU.add
                                     ).then_inc(*C.up("lru_scan", l, t))
                dve.wait_ge(*C.ago("lru_scan"))
                n = TOK if l == 0 else LAT
                V.tensor_tensor(Yv(l, 4 + t), f[:, 0:n], r[:, 0:n], ALU.add).then_inc(*C.up("lru_h", l, t))

            def conv(l, pairs):
                for t, k in pairs:
                    c = (l * CT + t) * TAPS + k
                    x = glu[:, t, 0:(2 if l == 0 else 1), k:k + LAT]
                    out = segs(Yv(l, t))
                    if k == 0:
                        dve.wait_ge(*C.ago("evac_dve"))
                        V.tensor_scalar(out, x, dwh[:, c:c + 1], at["dw_b"][:, l * CT + t:l * CT + t + 1], ALU.mult,
                                        ALU.add).then_inc(*C.up("conv", l, t, k))
                    else:
                        dve.wait_ge(*C.ago("conv", 1))
                        stt(out, x, dwh[:, c:c + 1], out, ALU.mult, ALU.add).then_inc(*C.up("conv", l, t, k))

            def att_max(l, s):
                kv, qb, isctx = groups(l)[s]
                k0 = LAT if isctx else 0
                h = l * HEADS + GROUP * kv
                dve.wait_ge(*C.at("scores", l, s))
                V.tensor_reduce(st[:, 0, :], psS[:, :, k0:TOK], axis=AX.X, op=ALU.max).then_inc(*C.up("att_max", l, s))
                dve.wait_ge(*C.ago("att_max"))
                stt(st[:, 1, :], st[:, 0, :], -SCALE, nsink[:, h:h + GROUP], ALU.mult, ALU.min).then_inc(*C.up("att_neg", l, s))
                dve.wait_ge(*C.ago("att_neg"))
                V.tensor_tensor(st[:, 3, :], st[:, 1, :], sink[:, h:h + GROUP], ALU.add).then_inc(*C.up("att_sn", l, s))

            def att_norm(l, s):
                isctx = groups(l)[s][2]
                k0 = LAT if isctx else 0
                dve.wait_ge(*C.at("att_es", l, s))
                V.tensor_tensor(st[:, 5, :], st[:, 2, :], st[:, 4, :], ALU.add).then_inc(*C.up("att_den", l, s))
                dve.wait_ge(*C.ago("att_den"))
                V.reciprocal(st[:, 5, :], st[:, 5, :]).then_inc(*C.up("att_den", l, s))
                dve.wait_ge(*C.ago("att_den"))
                for g in range(GROUP):
                    V.tensor_scalar(T[:, g, k0:TOK], T[:, g, k0:TOK], st[:, 5, g:g + 1], None, ALU.mult
                                    ).then_inc(*C.up("probs", l, s, g))

            def att_out(l, s):
                kv, qb, isctx = groups(l)[s]
                t0 = (LAT if isctx else 0) + qb * QB
                y = (Y if l == 0 else Y[:, :, LAT:TOK])[:, 8 + GROUP * kv:8 + GROUP * kv + GROUP, t0:t0 + QB]
                dve.wait_ge(*C.at("pv", l, s))
                stt(y, psS[:, 0, :].rearrange("p (g t) -> p g t", g=GROUP), 0.5, y, ALU.mult, ALU.mult
                    ).then_inc(*C.up("att_out", l, s))

            dve.wait_ge(*C.at("c_tanh"))
            stt(tiny[:, 0, :], tiny[:, 0, :], 1.0, at["c"], ALU.add, ALU.mult).then_inc(*C.up("cstat", 0))
            dve.wait_ge(*C.at("cstat_zero"))
            dve.wait_ge(*C.ago("cstat"))
            V.tensor_scalar(cstat[:, :, 0:2], tiny[:, 0, :].rearrange("p (k v) -> p k v", v=2), 0.5, None, ALU.mult
                            ).then_inc(*C.up("cstat", 1))
            n = LAYERS * 2 * CT
            dve.wait_ge(*C.at("lam_exp"))
            V.tensor_scalar(tiny[:, 1, 0:n], tiny[:, 1, 0:n], 1.0, None, ALU.add).then_inc(*C.up("lam_one"))
            V.tensor_scalar(tiny[:, 1, 16:16 + n], at["lam"], -1.0, 0.0, ALU.mult, ALU.max).then_inc(*C.up("derived"))
            dve.wait_ge(*C.at("lam_ln"))
            dve.wait_ge(*C.ago("derived"))
            V.tensor_tensor(tiny[:, 2, 0:n], tiny[:, 2, 0:n], tiny[:, 1, 16:16 + n], ALU.add).then_inc(*C.up("derived"))
            dve.wait_ge(*C.ago("derived"))
            for dst, src, f in ((s4, tiny[:, 2, 0:n], 4.0), (s4n, tiny[:, 2, 0:n], -4.0), (dwh, at["dw_w"], 0.5),
                                (hbr, at["b_r"], 0.5), (hbi, at["b_i"], 0.5), (lnhg, at["ln_g"], 0.5),
                                (lnhb, at["ln_b"], 0.5), (nsink, sink, -1.0)):
                V.tensor_scalar(dst, src, f, None, ALU.mult).then_inc(*C.up("derived"))
            dve.wait_ge(*C.ago("derived"))

            for m in range(DT):
                rms_add(0, m)
            for gb in range(GLOB):
                l, b = divmod(gb, NB)
                if b == 0:
                    if l:
                        rms_add(l, DT - 1)
                    rstd(l)
                    u0, n = unit(l, 0, 0), OPEN[l] // 2
                    if l == 0:
                        for quarter in range(4):
                            ada0_out(quarter)
                            h_quarter(l, quarter)
                            for i in range(n):
                                lo(u0 + n * quarter + i)
                    else:
                        for quarter in range(4):
                            h_quarter(l, quarter)
                            for i in range(n if 0 < quarter < 3 else 0):
                                lo(u0 + 4 + n * (quarter - 1) + i)
                        for a in PLAN[NB - 1]:
                            if a[2] == DT - 1:
                                ada_out(*a[:2])
                    for i in range(4):
                        lo(u0 + 2 * OPEN[l] + i)
                if b < OPEN[l]:
                    continue
                if b == B_OUT:
                    n = width(l, b)
                    for k in range(DT):
                        dve.wait_ge(*C.at("y_hi", l, k))
                        V.tensor_tensor(hl[:, k, 0:n], Yv(l, k), hh[:, k, 0:n].bitcast(F32), ALU.subtract
                                        ).then_inc(*C.up("y_lo", l, k))
                if gb + 2 < GLOB:
                    lo(2 * gb + 4)
                for a in (PLAN[b - 1] if l == 0 and b - 1 in PLAN else []):
                    if a[2] == DT - 1:
                        ada_out(*a[:2])
                if b - TP_LAG[l] - 1 in groups(l):
                    att_out(l, b - TP_LAG[l] - 1)
                if gb + 2 < GLOB:
                    lo(2 * gb + 5)
                evac(gb)
                if b in ROPE_AT[l]:
                    rope(l, ROPE_AT[l][b])
                if b in groups(l):
                    att_max(l, b)
                if b - 1 in LRU_AT[l]:
                    lru_v(l, LRU_AT[l].index(b - 1))
                if b - 2 in LRU_AT[l]:
                    lru_scan(l, LRU_AT[l].index(b - 2))
                if b in LRU_AT[l]:
                    taps(l, LRU_AT[l].index(b))
                conv(l, conv_taps(b))
                if b in groups(l):
                    att_norm(l, b)
                if b == LN_AT:
                    n = width(l, b)
                    dve.wait_ge(*C.at("ln_sum", l))
                    for t in range(CT):
                        stt(Yv(l, t), psM[:, 0:n], -1.0 / (CT * P), Yv(l, t), ALU.mult, ALU.add).then_inc(*C.up("ln_c", l, t))
                if b == LN_AT + 1:
                    n = width(l, b)
                    dve.wait_ge(*C.at("ln_std", l))
                    V.reciprocal(lnr[:, 0:n], lnr[:, 0:n]).then_inc(*C.up("ln_rstd", l))
                    dve.wait_ge(*C.ago("ln_rstd"))
                    for t in range(CT):
                        V.tensor_tensor(Yv(l, t), Yv(l, t), lnr[:, 0:n], ALU.mult).then_inc(*C.up("ln_n", l, t))
                if b == LN_AT + 2:
                    for t in range(CT):
                        c = l * CT + t
                        dve.wait_ge(*C.at("ln_th", l, t))
                        V.tensor_scalar(Yv(l, t), Yv(l, t), at["ln_g"][:, c:c + 1], at["ln_b"][:, c:c + 1], ALU.mult,
                                        ALU.add).then_inc(*C.up("ln_z", l, t))
                    for t in range(CT):
                        dve.wait_ge(*C.ago("ln_z", CT - 1 - t))
                        stt(segs(Yv(l, t)), glu_in(l, t), 1.0, segs(Yv(l, t)), ALU.add, ALU.mult).then_inc(*C.up("ln_y", l, t))

                if b > B_OUT:
                    rms_add(l + 1, b - B_OUT - 1)

            rms_add(LAYERS, DT - 1)
            rstd(LAYERS)
            dve.wait_ge(*C.ago("evac_dve"))
            for m in range(DT):
                stt(Y[:, m, 0:LAT], Y[:, m, 0:LAT], at["final_g"][:, m:m + 1], tbuf[:, 0:LAT], ALU.mult, ALU.mult
                    ).then_inc(*C.up("final", m))
        return dict(C.marks)


def _tables():
    ident = np.eye(P, dtype=np.float32)
    perm = np.zeros((P, P), np.float32)
    for m in range(P):
        perm[m + 32 if m % 64 < 32 else m - 32, m] = -1.0 if m % 64 < 32 else 1.0
    half = HD // 2
    inv = np.float32(10000.0) ** (-np.arange(0, half, 2, dtype=np.float32) / np.float32(half))
    t = np.arange(LAT)
    row, col = (t // 64).astype(np.float32), (t % 64).astype(np.float32)
    ang = np.concatenate([row[:, None] * inv, row[:, None] * inv, col[:, None] * inv, col[:, None] * inv], axis=1).T
    a, b = np.arange(P)[None, :], np.arange(P)[:, None]
    mask = np.stack([np.where(a > b, MASKED, 0.0), np.where(a < b, MASKED, 0.0)], axis=1).astype(np.float32)
    return {"ident": ident, "ones": np.ones((P, P), np.float32), "perm": perm,
            "cos": np.cos(ang).astype(np.float32), "sin": np.sin(ang).astype(np.float32), "mask": mask}


def _lay_out(x, c, ctx, c_ctx, norm_g, w_ada, b_ada, w_in, dw_w, dw_b, ln_g, ln_b, pw_w, pw_b, lru_conv_w,
             lru_conv_b, lru_w_r, lru_b_r, lru_w_i, lru_b_i, lru_lam, attn_sink, w_out, final_g):
    def cols(a):
        a = a.reshape(*a.shape[:-1], -1, P)
        return np.moveaxis(a, -1, 0).reshape(P, -1)

    small = _tables()
    small.update(
        c=np.stack([c[0].reshape(DT, P).T, c_ctx.reshape(DT, P).T], axis=2), norm_g=cols(norm_g), final_g=cols(final_g),
        b_ada=cols(b_ada), dw_w=np.moveaxis(dw_w.reshape(LAYERS, TAPS, CT, P), (3, 0, 2, 1), (0, 1, 2, 3)),
        dw_b=cols(dw_b), ln_g=cols(ln_g), ln_b=cols(ln_b), pw_b=cols(pw_b),
        lcw=lru_conv_w.reshape(LAYERS, 2, LTAPS, CT, P).transpose(4, 0, 1, 3, 2), lcb=cols(lru_conv_b),
        b_r=cols(lru_b_r), b_i=cols(lru_b_i), lam=cols(lru_lam),
        sink=np.broadcast_to(attn_sink.reshape(1, -1), (P, LAYERS * HEADS)))
    packed = np.concatenate([np.ascontiguousarray(small[name]).reshape(P, n) for name, n in SMALL], axis=1)
    blocks = []
    for l in range(LAYERS):
        for kind, i in BLOCKS:
            w, at = (w_out[l], i * P) if kind == "out" else (w_in[l], COLUMN[kind] + i * P)
            blocks.append(w[:, at:at + P].reshape(DT, P, P).transpose(1, 0, 2).reshape(P, DT * P))
    lru = np.stack([lru_w_r, lru_w_i], axis=1)
    lru = lru.reshape(LAYERS, 2, 2, CT, 2, 64, 64).transpose(0, 1, 4, 5, 2, 3, 6).reshape(LAYERS, 2, 2, 64, 2 * CT, 64)
    tokens = np.concatenate([x[0], ctx[0]], axis=0)
    return {
        "small": packed, "w_blocks": np.stack(blocks), "w_ada": w_ada,
        "pw": pw_w.reshape(LAYERS, CT, P, CT, P).transpose(0, 2, 3, 1, 4).reshape(LAYERS, P, CT * CT * P),
        "lru_w": lru, "xT": tokens.T.reshape(DT, P, TOK).transpose(1, 0, 2),
    }


def kernel(**inputs):
    import concourse.bacc as bacc
    from concourse.bass_utils import run_bass_kernel_spmd

    arrays = {n: np.ascontiguousarray(a) for n, a in _lay_out(**{n: np.asarray(a) for n, a in inputs.items()}).items()}

    def build(known):
        nc = bacc.Bacc("TRN2", target_bir_lowering=False, num_devices=1, dynamic_dma_scratch_size=64)
        io = {n: nc.dram_tensor("in_" + n, a.shape, mybir.dt.from_np(a.dtype), kind="ExternalInput").ap()
              for n, a in arrays.items()}
        io["out"] = nc.dram_tensor("out", (P, DT, LAT), F32, kind="ExternalOutput").ap()
        return nc, program(nc, io, known)

    marks = build({})[1]
    nc = build(marks)[0]
    r = run_bass_kernel_spmd(nc, [{"in_" + n: a for n, a in arrays.items()}], core_ids=[0])
    return r.results[0]["out"].transpose(1, 0, 2).reshape(D, LAT).T.reshape(1, LAT, D)
```

```python
from contextlib import ExitStack

import numpy as np
import concourse.bass as bass
from concourse import mybir

F32 = mybir.dt.float32
F32R = mybir.dt.float32r
ACT = mybir.ActivationFunctionType
ALU = mybir.AluOpType
AX = mybir.AxisListType

P = 128
D = 2048
DT = D // P
LAT, CTX = 256, 256
TOK = LAT + CTX
LAYERS = 2
HD = 128
HEADS, KV_HEADS, GROUP = 8, 2, 4
SCALE = HD ** -0.5
QB = 128
TAPS = 31
PAD = TAPS // 2
LTAPS = 4
CT = 4
EPS = 1e-6
ADA_KINDS = 3
SHIFT, SCL, GATE = range(3)
MASKED = -1e30

KV = [("k", i) for i in range(KV_HEADS)] + [("v", i) for i in range(KV_HEADS)]
GLU = [(s, t) for t in range(CT) for s in ("b", "a")]
REST = ([("q", h) for h in range(4)] + [("ag", h) for h in range(4)]
        + [("q", h) for h in range(4, 8)] + [("ag", h) for h in range(4, 8)]
        + [("lg", t) for t in range(CT)] + [("cg", t) for t in range(CT)]
        + [("out", m) for m in range(DT)])
BLOCKS = [[("x", t) for t in range(CT)] + first + REST for first in (KV + GLU, GLU + KV)]
NB = len(BLOCKS[0])
B_OUT = NB - DT
B_Q = BLOCKS[0].index(("q", 0))
COLUMN = {"x": 0, "k": 512, "v": 768, "a": 1024, "b": 1536, "cg": 2048, "lg": 2560, "q": 3072, "ag": 4096}
BOTH = "xkv"

OPEN = [7, 4]
SIDE = [6, 4]
QT = DT // 4
FINAL = 4
HALF = DT // 2 * P

LRU_TAPS = [[7, 9, 11, 13], [4, 7, 10, 13]]
LRU_MM = [[8, 10, 12, 14], [6, 9, 12, 14]]
LRU_SCAN = [[9, 11, 13, 15], [7, 10, 13, 15]]
CONV_AT = [12, 8]
CONV_TAPS = [[4, 3, 2, 3, 3, 4, 3, 3, 3, 3, 4, 3, 3, 3, 3, 3, 3, 3, 3, 3],
             [3, 0, 2, 3, 3, 8, 6, 3, 1, 2, 3, 2, 1, 3, 2, 4, 4, 1, 2, 3, 3, 3]]
LN_SUM, LN_VAR, LN_ACT = [32, 31], [33, 33], [34, 34]
PW_AT = 35
LAST_GROUPS = [22, 25, 29, 32]
TP_LAG = [1, 2]
ROPE_AT = [{9: 4, 10: 5, 17: 16, 18: 17, 19: 18, 20: 19, 25: 24, 26: 25, 27: 26, 28: 27},
           {13: 12, 14: 13, 17: 16, 18: 17, 19: 18, 20: 19, 25: 24, 26: 25, 27: 26, 28: 27}]


def groups(l):
    if l == 0:
        out, s = {}, 22
        for kv in range(KV_HEADS):
            for ctx in (False, True):
                for qb in range(2):
                    out[s] = (kv, qb, ctx)
                    s += 2
        return out
    return {s: (kv, qb, False) for s, (kv, qb) in zip(LAST_GROUPS, ((0, 0), (0, 1), (1, 0), (1, 1)))}


SMALL = [("c", DT * 2), ("ones", P), ("perm", P), ("cos", LAT), ("sin", LAT),
         ("norm_g", LAYERS * DT), ("final_g", DT), ("b_ada", LAYERS * ADA_KINDS * DT), ("dw_w", LAYERS * CT * TAPS),
         ("dw_b", LAYERS * CT), ("ln_g", LAYERS * CT), ("ln_b", LAYERS * CT), ("pw_b", LAYERS * CT),
         ("lcw", LAYERS * 2 * CT * LTAPS), ("lcb", LAYERS * 2 * CT), ("b_r", LAYERS * 2 * CT),
         ("b_i", LAYERS * 2 * CT), ("lam", LAYERS * 2 * CT), ("sink", LAYERS * HEADS)]
N_SMALL = sum(n for _, n in SMALL)


def ada_plan():
    rest = [(0, GATE, k) for k in range(DT)] + [(1, kind, k) for kind in (SHIFT, SCL, GATE) for k in range(DT)]
    count = {b: 1 for b in range(OPEN[0], NB)}
    count.update({B_OUT - 1: 2, NB - 1: 2, NB: 2})
    for b in range(OPEN[0], OPEN[0] + len(rest) - sum(count.values())):
        count[b] = 2
    plan = {b: [rest.pop(0) for _ in range(n)] for b, n in count.items()}
    assert not rest
    return plan


ADA0 = [("ada0", kind, quarter, g) for quarter in range(4) for kind in (SCL, SHIFT) for g in range(4)]
LEAD = 3
TP_SLOT = 9 - LEAD


def opening(l, quarter):
    return [("open", l, quarter, b, min(4, SIDE[l] - b)) for b in range(0, SIDE[l], 4)]


def opening_units(l):
    units = []
    for quarter in range(4):
        units += [(quarter, pair) for pair in range(SIDE[l] // 2)]
        if quarter > 1:
            units += [("half", l, b, quarter - 2) for b in range(SIDE[l], OPEN[l])]
    return units


def unit(l, b, j):
    return 2 * (l * NB + b) + j


def open_unit(l, *which):
    return unit(l, 0, 0) + opening_units(l).index(which)


def block_unit(gb, j):
    l, b = divmod(gb, NB)
    return open_unit(l, "half", l, b, j) if b < OPEN[l] else unit(l, b, j)


def stream():
    plan = ada_plan()
    s = ADA0[:8 + LEAD]
    for quarter in range(4):
        s += opening(0, quarter) + [u for u in opening_units(0) if u[0] == "half" and u[3] == quarter - 2]
        s += ADA0[8 + LEAD + 8 * quarter:8 + LEAD + 8 * (quarter + 1)]
    s += [("w", b) for b in (OPEN[0], OPEN[0] + 1)]
    for l in range(LAYERS):
        for b in range(OPEN[l], NB):
            if b == PW_AT:
                s.append(("pw", l))
            if b + 2 < NB:
                s.append(("w", l * NB + b + 2))
            elif b + 2 == NB and l + 1 < LAYERS:
                s += opening(l + 1, 0)
            elif l + 1 < LAYERS:
                s += opening(l + 1, 1)
            if l == 0:
                s += [("ada", *a) for a in plan[b]]
        if l + 1 < LAYERS:
            s += [("ada", *a) for a in plan[NB]]
            s += opening(l + 1, 2) + opening(l + 1, 3)
            s += [("w", (l + 1) * NB + b) for b in (OPEN[l + 1], OPEN[l + 1] + 1)]
    return s


class Counts:

    def __init__(self, nc, ctx, known):
        self.nc, self.ctx, self.known = nc, ctx, known
        self.sems, self.n, self.marks = {}, {}, {}

    def sem(self, name):
        if name not in self.sems:
            self.sems[name] = self.ctx.enter_context(self.nc.semaphore(name))
            self.n[name] = 0
        return self.sems[name]

    def up(self, name, *key, by=1):
        s = self.sem(name)
        self.n[name] += by
        self.marks[(name, *key)] = self.n[name]
        return s, by

    def at(self, name, *key):
        return self.sem(name), self.known[(name, *key)] if self.known else 1

    def ago(self, name, n=0):
        return self.sem(name), self.n[name] - n


def program(nc, io, known):
    ctx = ExitStack()
    with ctx:
        def sb(name, shape, dt=F32):
            return ctx.enter_context(nc.sbuf_tensor(name, shape, dt))

        def pb(name, shape):
            return ctx.enter_context(nc.psum_tensor(name, shape, F32))

        NRAW = 3
        hh = sb("h_hi", [P, DT, TOK], F32R)
        hl = sb("h_lo", [P, DT, TOK], F32R)
        Y = sb("Y", [P, DT, TOK])
        raw = sb("raw", [P, NRAW, DT * P])
        wh = sb("w_hi", [P, 4, DT // 2 * P], F32R)
        wl = sb("w_lo", [P, 4, DT // 2 * P], F32R)
        T = sb("T", [P, 8, TOK])
        glu = sb("glu", [P, CT, 2, PAD + LAT + PAD])
        qreg = sb("qreg", [P, HEADS * TOK])
        kT = sb("kT", [P, KV_HEADS, TOK])
        v = sb("v", [P, 4, KV_HEADS * HD])
        bd = sb("bd", [P, 2, 2 * CT, P])
        tbuf = sb("tbuf", [P, TOK])
        lnr = sb("lnr", [P, TOK])
        cstat = sb("cstat", [P, DT, 34])
        adasb = lnr
        small = sb("small", [P, N_SMALL])
        der = sb("der", [P, LAYERS * (2 * 2 * CT + 2 * CT + HEADS)])
        ada = sb("ada", [P, LAYERS, 2, ADA_KINDS * DT])
        A = sb("A", [P, LAYERS, 2, DT])
        st = sb("stats", [P, 6, 4])
        eps = sb("eps", [P, 1])
        rounded = sb("rounded", [P, 3, P], F32R)
        tiny = sb("tiny", [P, 3, 32])

        pB = [pb(f"psum_block{i}", [P, TOK]) for i in range(2)]
        psA = pb("psum_ada", [P, TOK])
        psM = pb("psum_misc", [P, TOK])
        psS = pb("psum_scores", [P, 4, TOK])

        q = qreg[:, :].rearrange("p (h t) -> p h t", h=HEADS)
        LW = LTAPS - 1 + LAT + LTAPS - 1
        lrux = qreg[:, HEADS * TOK - CT * 2 * LW:].rearrange("p (t s w) -> p t s w", t=CT, s=2)

        at = {}
        o = 0
        for name, n in SMALL:
            at[name] = small[:, o:o + n]
            o += n
        cT = at["c"].rearrange("p (k v) -> p k v", v=2)
        ident, ones, perm = rounded[:, 0, :].bitcast(F32), at["ones"], at["perm"]
        cos, sin = at["cos"], at["sin"]
        norm_g = at["norm_g"].rearrange("p (l k) -> p l k", l=LAYERS)
        b_ada = at["b_ada"].rearrange("p (l k) -> p l k", l=LAYERS)
        lcw = at["lcw"].rearrange("p (n k) -> p n k", k=LTAPS)
        sink = at["sink"]

        d0 = [0]

        def cut(n):
            d0[0] += n
            return der[:, d0[0] - n:d0[0]]

        dwh = at["dw_w"]
        hbr, hbi = at["b_r"], at["b_i"]
        s4n, s4 = cut(LAYERS * 2 * CT), cut(LAYERS * 2 * CT)
        lnhg, lnhb = cut(LAYERS * CT), cut(LAYERS * CT)
        nsink = cut(LAYERS * HEADS)

        C = Counts(nc, ctx, known)
        STREAM = stream()
        where = {s: i for i, s in enumerate(STREAM)}
        PLAN = ada_plan()
        GLOB = LAYERS * NB

        opened = where["w", OPEN[0]]
        SLOT = [i % (NRAW + 1) if i < opened else (i - opened) % NRAW for i in range(len(STREAM))]

        def arrived(item):
            i = where[item]
            return C.sem(f"raw{SLOT[i]}"), 16 * SLOT[:i + 1].count(SLOT[i])

        def slot(i):
            return glu[:, :, :, :].rearrange("p t s w -> p (t s w)")[:, 0:DT * P] if SLOT[i] == NRAW else raw[:, SLOT[i], :]

        def raw_of(item):
            return slot(where[item])

        def used(i):
            item = STREAM[i]
            if item[0] == "w":
                return C.at("lo", 2 * item[1] + 1)
            if item[0] == "open":
                return C.at("lo", open_unit(item[1], item[2], (item[3] + item[4]) // 2 - 1))
            if item[0] == "half":
                return C.at("lo", open_unit(item[1], *item))
            if item[0] == "pw":
                return C.at("pw_mm", item[1], CT - 1)
            return C.at(item[0] + "_mm", *item[1:])

        def source(u):
            l, r = divmod(u, 2 * NB)
            if r < 2 * OPEN[l]:
                item = opening_units(l)[r]
                if item[0] == "half":
                    return item, 0
                return opening(l, item[0])[item[1] // 2], item[1] % 2
            return ("w", l * NB + r // 2), r % 2

        def block_done(gb):
            l, b = divmod(gb, NB)
            return C.at("mm", open_unit(l, 3, b // 2) if b < SIDE[l] else block_unit(gb, 1))

        def bank(gb):
            l, b = divmod(gb, NB)
            if SIDE[l] <= b < OPEN[l]:
                return psM[:, :]
            return psS[:, b - 2, :] if 2 <= b < SIDE[l] else pB[gb % 2][:, :]

        def k_tile(b, i):
            return (i + CT) % DT if b >= B_OUT else i

        def y_parts(l):
            return slice(0, TOK) if l == 0 else slice(LAT, TOK)

        def y_at(l, b):
            order = [k_tile(B_OUT, i) for i in range(DT)]
            if l == 0 and b >= B_OUT - 1:
                return order[:CT] if b < B_OUT else order[CT:] if b == B_OUT else []
            if b == B_OUT:
                return list(range(CT))
            if l and b in (B_OUT - 3, B_OUT - 2):
                half = (DT - CT) // 2
                return list(range(CT + (b - B_OUT + 3) * half, CT + (b - B_OUT + 4) * half))
            return []

        def done_before(l, b):
            last = PLAN.get(b - 1, []) if l == 0 else PLAN[NB] if b == OPEN[l] else []
            return [a[:2] for a in last if a[2] == DT - 1]

        def width(l, b):
            return TOK if l == 0 or BLOCKS[l][b][0] in BOTH else LAT

        def Yv(l, m):
            return Y[:, m, :] if l == 0 else Y[:, m, LAT:TOK]

        def segs(ap):
            return ap.rearrange("p (s t) -> p s t", t=LAT)

        def glu_in(l, t):
            return glu[:, t, 0:(2 if l == 0 else 1), PAD:PAD + LAT]

        def released(gb):
            kind = BLOCKS[gb // NB][gb % NB][0]
            return C.at("evac_act" if kind in "xkvbq" else "evac_dve", gb)

        def pw_bank(l, m):
            return psM if m % 2 == 0 else pB[(l * NB + PW_AT + 1) % 2]

        def conv_taps(l, b):
            plan = CONV_TAPS[l]
            assert sum(plan) == TAPS * CT // 2
            if not 0 <= b - CONV_AT[l] < len(plan):
                return []
            first = sum(plan[:b - CONV_AT[l]])
            return [(2 * (n // TAPS) + i, n % TAPS) for n in range(first, first + plan[b - CONV_AT[l]]) for i in range(2)]

        block = ctx.enter_context(nc.Block())

        @block.sync
        def _(sp):
            sp.dma_start(small[:, :], io["small"]).then_inc(*C.up("small_in", by=16))
            sp.dma_start(T[:, 5, 0:3 * P], io["exact"]).then_inc(*C.up("exact_in", by=16))

            def gate_weights(l):
                if l:
                    sp.wait_ge(*C.at("lru_mm", l - 1, CT - 1))
                else:
                    sp.wait_ge(*C.at("bd_zero"))
                for g in range(2):
                    for j in range(2):
                        sp.dma_start(bd[64 * j:64 * j + 64, g, :, 64 * j:64 * j + 64],
                                     io["lru_w"][l, g, j]).then_inc(*C.up("bd_in", l, g, j, by=16))

            def residual(m):
                if m < 2:
                    sp.wait_ge(*C.at("att_out", 0, max(groups(0))))
                else:
                    sp.wait_ge(*C.at("evac_dve", B_OUT + m - 2))
                sp.dma_start(T[:, m % 2, :], io["xT"][:, m, :]).then_inc(*C.up(f"xs{m % 2}", m, by=16))

            for i, item in enumerate(STREAM):
                if SLOT[i] in SLOT[:i]:
                    sp.wait_ge(*used(i - 1 - SLOT[:i][::-1].index(SLOT[i])))
                dst = slot(i)
                if item[0] == "w":
                    src = io["w_blocks"][item[1]]
                elif item[0] == "open":
                    l, quarter, b, n = item[1:]
                    src = io["w_blocks"][l * NB + b:l * NB + b + n, :, quarter * QT * P:(quarter + 1) * QT * P
                                         ].rearrange("b p c -> p b c")
                    dst = dst[:, 0:n * QT * P].rearrange("p (b c) -> p b c", b=n)
                elif item[0] == "half":
                    l, b, j = item[1:]
                    src = io["w_blocks"][l * NB + b, :, j * HALF:(j + 1) * HALF]
                    dst = dst[:, 0:HALF]
                elif item[0] == "ada0":
                    kind, quarter, g = item[1:]
                    at = kind * D + quarter * QT * P
                    src = io["w_ada"][0, g * QT * P:(g + 1) * QT * P, at:at + QT * P].rearrange("(j p) c -> p j c", p=P)
                    dst = dst.rearrange("p (j c) -> p j c", j=QT)
                elif item[0] == "pw":
                    src = io["pw"][item[1]]
                else:
                    l, kind, k = item[1:]
                    src = io["w_ada"][l, k * P:(k + 1) * P, kind * D:(kind + 1) * D]
                sp.dma_start(dst, src).then_inc(C.sem(f"raw{SLOT[i]}"), 16)
                if 2 <= i < 6:
                    g = i - 2
                    sp.dma_start(Y[:, 4 * g:4 * g + 4, :], io["xT"][:, 4 * g:4 * g + 4, :]
                                 ).then_inc(*C.up(f"x_in{g}", by=16))
                if i == 2 * DT:
                    gate_weights(0)
                if item == ("w", B_OUT):
                    gate_weights(1)
                if item[0] == "w" and 0 <= item[1] - B_OUT - 2 < DT - 2:
                    residual(item[1] - B_OUT - 2)
                elif item[:2] == ("open", 1) and item[2] < 2:
                    residual(DT - 2 + item[2])
            for m in range(0, DT, FINAL):
                sp.wait_ge(*C.at("final", m))
                sp.dma_start(io["out"][:, m:m + FINAL, :], Y[:, m:m + FINAL, 0:LAT]).then_inc(*C.up("stored", by=16))
            sp.wait_ge(*C.ago("stored"))

        @block.gpsimd
        def _(pool):
            nc.gpsimd.memset(cstat[:, :, :], 0.0).then_inc(*C.up("cstat_zero"))
            nc.gpsimd.memset(eps[:, :], EPS).then_inc(*C.up("eps_set"))
            nc.gpsimd.memset(bd[:, :, :, :], 0.0).then_inc(*C.up("bd_zero"))
            for l in range(LAYERS):
                if l:
                    pool.wait_ge(*C.at("scores", l - 1, max(groups(l - 1))))
                nc.gpsimd.memset(lrux[:, :, :, :], 0.0).then_inc(*C.up("lrux_zero", l))
                if l == 0:
                    pool.wait_ge(*used(max(i for i in range(opened) if SLOT[i] == NRAW)))
                    nc.gpsimd.memset(glu[:, :, :, :], 0.0).then_inc(*C.up("glu_zero"))

        @block.tensor
        def _(pe):
            mm = nc.tensor.matmul

            def ada_mm(l, kind, k):
                pe.wait_ge(*arrived(("ada", l, kind, k)))
                w = raw_of(("ada", l, kind, k))
                if k == 0:
                    pe.wait_ge(*(C.at("ada_out", *before(l, kind)) if (l, kind) != (0, GATE) else C.at("ada0_sum", SHIFT, 3)))
                for j in range(4):
                    last = mm(psA[32 * j:32 * j + 32, :], cstat[:, k, 2:34], w[:, j * TOK:(j + 1) * TOK],
                              start=(k == 0), stop=(k == DT - 1), tile_position=(0, 32 * j))
                last.then_inc(*C.up("ada_mm", l, kind, k))

            def ada_tp(l, kind):
                pe.wait_ge(*C.at("ada_rows", l, kind))
                for j in range(4):
                    last = nc.tensor.transpose(psA[:, j * P:(j + 1) * P], adasb[:, j * P:(j + 1) * P], ident)
                last.then_inc(*C.up("ada_tp", l, kind))

            def ada0_mm(kind, quarter, g):
                pe.wait_ge(*arrived(("ada0", kind, quarter, g)))
                w = raw_of(("ada0", kind, quarter, g))
                rows = cstat[:, :, 2:34] if kind == SCL else cstat[:, :, 0:32]
                if g == 0 and kind == SCL and quarter:
                    pe.wait_ge(*C.at("ada0_sum", SHIFT, quarter - 1))
                for j in range(4):
                    last = mm(psA[32 * j:32 * j + 32, :], rows[:, g * QT + j, :], w[:, j * TOK:(j + 1) * TOK],
                              start=(kind == SCL and g == 0), stop=(kind == SHIFT and g == 3), tile_position=(0, 32 * j))
                last.then_inc(*C.up("ada0_mm", kind, quarter, g))

            def ada0_tp(quarter):
                pe.wait_ge(*C.at("ada0_rows", quarter))
                for j in range(4):
                    last = nc.tensor.transpose(psA[:, j * P:(j + 1) * P], T[:, 6, j * P:(j + 1) * P], ident)
                last.then_inc(*C.up("ada0_tp", quarter))

            def rms_mm(l):
                n = TOK if l < LAYERS else LAT
                pe.wait_ge(*C.at("rms_add", l, DT - 2))
                mm(psS[:, 0, 0:n], ones, T[:, 4, 0:n], start=True, stop=False)
                pe.wait_ge(*C.at("rms_sq", l, DT - 1))
                mm(psS[:, 0, 0:n], ones, T[:, 2 + (DT - 1) % 2, 0:n], start=False, stop=True).then_inc(*C.up("rms_mm", l))

            def mm_open(l, quarter, pair):
                u = open_unit(l, quarter, pair)
                pe.wait_ge(*C.at("lo", u))
                for b in (2 * pair, 2 * pair + 1):
                    if quarter == 0:
                        if l and b < 2:
                            pe.wait_ge(*released(l * NB + b - 2))
                        elif b == 2:
                            pe.wait_ge(*C.at("rms_std", l))
                for i in range(QT):
                    k = quarter * QT + i
                    if pair == 0:
                        pe.wait_ge(*C.at("h_lo", l, k))
                    for c, b in enumerate((2 * pair, 2 * pair + 1)):
                        ps = bank(l * NB + b)
                        at = (c * QT + i) * P
                        hi, lo = wh[:, u % 4, at:at + P], wl[:, u % 4, at:at + P]
                        mm(ps, hi, hh[:, k, :], start=(k == 0), stop=False)
                        mm(ps, hi, hl[:, k, :], start=False, stop=False)
                        last = mm(ps, lo, hh[:, k, :], start=False, stop=(k == DT - 1))
                    if i == QT - 1:
                        last.then_inc(*C.up("mm", u))
                    if l == 0 and quarter < 3:
                        slot = pair * QT + i
                        if slot < 8 - LEAD:
                            ada0_mm(*ADA0[8 * quarter + 8 + LEAD + slot][1:])
                        elif slot == TP_SLOT:
                            ada0_tp(quarter + 1)
                        elif quarter < 2 and TP_SLOT + 1 < slot < TP_SLOT + 2 + LEAD:
                            ada0_mm(*ADA0[8 * quarter + 16 + slot - TP_SLOT - 2][1:])

            def mm_half(gb, j):
                l, b = divmod(gb, NB)
                n = width(l, b)
                ps = bank(gb)
                u = block_unit(gb, j)
                pe.wait_ge(*C.at("lo", u))
                if j == 0 and b == PW_AT + 1:
                    pe.wait_ge(*C.at("pw_out", l, CT - 1))
                elif j == 0 and b >= OPEN[l]:
                    pe.wait_ge(*released(gb - 2 if b - 2 >= OPEN[l] else l * NB + b % 2))
                slot = u % 4
                t = y_parts(l) if b >= B_OUT else slice(0, n)
                for i in range(DT // 2):
                    at = j * DT // 2 + i
                    k = k_tile(b, at)
                    if b == B_OUT:
                        pe.wait_ge(*C.at("y_lo", l, k))
                    hi, lo = wh[:, slot, i * P:(i + 1) * P], wl[:, slot, i * P:(i + 1) * P]
                    mm(ps[:, 0:n], hi, hh[:, k, t], start=(at == 0), stop=False)
                    mm(ps[:, 0:n], hi, hl[:, k, t], start=False, stop=False)
                    last = mm(ps[:, 0:n], lo, hh[:, k, t], start=False, stop=(at == DT - 1))
                last.then_inc(*C.up("mm", u))

            def rope_mm(l, b):
                kind, i = BLOCKS[l][b]
                if not misc:
                    pe.wait_ge(*C.at("evac_act", OPEN[0] - 1))
                pe.wait_ge(*C.at("evac_act", l * NB + b))
                misc_free(l)
                src = kT[:, i, 0:LAT] if kind == "k" else q[:, i, 0:LAT]
                mm(psM[:, 0:LAT], perm, src, start=True, stop=True).then_inc(*C.up("rope_mm", l, kind, i))

            def misc_free(l):
                if misc:
                    pe.wait_ge(*C.at(*misc[-1]))

            misc = []
            scores_free = []

            def lru_mm(l, t):
                pe.wait_ge(*C.at("taps", l, t, 1))
                if t == 0:
                    pe.wait_ge(*C.at("bd_in", l, 1, 1))
                    for b in range(2, SIDE[l]):
                        pe.wait_ge(*C.at("evac_act", l * NB + b))
                else:
                    pe.wait_ge(*C.at("lru_tanh", l, t - 1, 1))
                for d in range(2):
                    for g in range(2):
                        last = mm(psS[:, 2 * d + g, :], bd[:, g, d * CT + t, :], T[:, 4 * d, :], start=True, stop=True)
                last.then_inc(*C.up("lru_mm", l, t))

            def scores(l, s):
                kv, qb, isctx = groups(l)[s]
                pe.wait_ge(*C.at("rope", l, "k", KV_HEADS - 1))
                if isctx:
                    pe.wait_ge(*C.at("evac_act", l * NB + 16 + 8 * kv + 3))
                else:
                    pe.wait_ge(*C.at("rope", l, "q", GROUP * kv + GROUP - 1))
                if scores_free:
                    pe.wait_ge(*C.at("att_out", l, scores_free[-1]))
                else:
                    pe.wait_ge(*C.at("lru_tanh", l, CT - 1, 1))
                t0 = (LAT if isctx else 0) + qb * QB
                for g in range(GROUP):
                    qt = q[:, GROUP * kv + g, t0:t0 + QB]
                    if isctx:
                        last = mm(psS[:, g, LAT:TOK], qt, kT[:, kv, LAT:TOK], start=True, stop=True)
                    else:
                        mm(psS[:, g, :], qt, kT[:, kv, :], start=True, stop=False)
                        far = (1 - qb) * QB
                        last = mm(psS[:, g, far:far + QB], rounded[:, 0, :], rounded[:, 1 + qb, :],
                                  start=False, stop=True)
                last.then_inc(*C.up("scores", l, s))
                scores_free.append(s)

            def p_tp(l, s):
                isctx = groups(l)[s][2]
                for g in range(GROUP):
                    pe.wait_ge(*C.at("probs", l, s, g))
                    for kt in range(2 if isctx else 0, 4):
                        last = nc.tensor.transpose(psS[:, g, kt * P:(kt + 1) * P], T[:, g, kt * P:(kt + 1) * P], ident)
                    last.then_inc(*C.up("p_tp", l, s, g))

            def pv(l, s):
                kv, qb, isctx = groups(l)[s]
                pe.wait_ge(*C.at("pT", l, s, GROUP - 1))
                pe.wait_ge(*C.at("v_out", l, KV_HEADS - 1))
                first = 2 if isctx else 0
                for kt in range(first, 4):
                    last = mm(psS[:, 0, :], v[:, kt, kv * HD:(kv + 1) * HD], T[:, 4 + kt, :],
                              start=(kt == first), stop=(kt == 3))
                last.then_inc(*C.up("pv", l, s))

            def ln_mm(l, stage):
                n = TOK if l == 0 else LAT
                misc_free(l)
                pe.wait_ge(*C.at("ln_add", l, stage))
                mm(psM[:, 0:n], ones, lnr[:, 0:n], start=True, stop=True).then_inc(*C.up(stage, l))
                misc.append(("ln_c", l, CT - 1) if stage == "ln_sum" else ("ln_std", l))

            def pw_mm(l, m):
                n = TOK if l == 0 else LAT
                if m < 2:
                    misc_free(l)
                    pe.wait_ge(*released(l * NB + PW_AT - 1))
                else:
                    pe.wait_ge(*C.at("pw_out", l, m - 2))
                if m == 0:
                    pe.wait_ge(*arrived(("pw", l)))
                w = raw_of(("pw", l)).rearrange("p (m k c) -> p m k c", m=CT, k=CT)
                for k in range(CT):
                    if m == 0:
                        pe.wait_ge(*C.at("ln_y", l, k))
                    last = mm(pw_bank(l, m)[:, 0:n], w[:, m, k, :], Yv(l, k), start=(k == 0), stop=(k == CT - 1))
                last.then_inc(*C.up("pw_mm", l, m))

            order = [(0, GATE), (1, SHIFT), (1, SCL), (1, GATE)]

            def before(l, kind):
                return order[order.index((l, kind)) - 1]

            pe.wait_ge(*C.at("small_in"))
            pe.wait_ge(*C.at("rounded"))
            pe.wait_ge(*C.at("cstat", 1))
            for item in ADA0[:8]:
                ada0_mm(*item[1:])
            ada0_tp(0)
            rms_mm(0)
            for item in ADA0[8:8 + LEAD]:
                ada0_mm(*item[1:])

            for gb in range(GLOB):
                l, b = divmod(gb, NB)
                if b == 0:
                    scores_free.clear()
                    if l:
                        rms_mm(l)
                        for a in PLAN[NB]:
                            ada_mm(*a)
                    for quarter in range(4):
                        for pair in range(SIDE[l] // 2):
                            mm_open(l, quarter, pair)
                        for c in range(SIDE[l], OPEN[l] if quarter > 1 else 0):
                            mm_half(l * NB + c, quarter - 2)
                if b < OPEN[l]:
                    continue
                mm_half(gb, 0)
                for a in done_before(l, b):
                    ada_tp(*a)
                if b - TP_LAG[l] - 1 in groups(l):
                    pv(l, b - TP_LAG[l] - 1)
                mm_half(gb, 1)
                if b in ROPE_AT[l]:
                    rope_mm(l, ROPE_AT[l][b])
                    misc.append(("rope_t", l, *BLOCKS[l][ROPE_AT[l][b]]))
                if b and BLOCKS[l][b - 1][0] == "v":
                    i = BLOCKS[l][b - 1][1]
                    pe.wait_ge(*C.at("evac_act", gb - 1))
                    misc_free(l)
                    for kt in range(4):
                        last = nc.tensor.transpose(psM[:, kt * P:(kt + 1) * P], tbuf[:, kt * P:(kt + 1) * P], ident)
                    last.then_inc(*C.up("v_tp", l, i))
                    misc.append(("v_out", l, i))
                if b in LRU_MM[l]:
                    lru_mm(l, LRU_MM[l].index(b))
                if b in groups(l):
                    scores(l, b)
                if b - TP_LAG[l] in groups(l):
                    p_tp(l, b - TP_LAG[l])
                if b == LN_SUM[l]:
                    ln_mm(l, "ln_sum")
                if b == LN_VAR[l]:
                    ln_mm(l, "ln_var")
                if b == PW_AT:
                    for m in range(CT):
                        pw_mm(l, m)
                    misc.append(("pw_out", l, CT - 1))
                if l == 0:
                    for a in PLAN[b]:
                        ada_mm(*a)
            rms_mm(LAYERS)

        @block.scalar
        def _(act):
            fn = nc.scalar.activation

            def hi(u):
                item, j = source(u)
                act.wait_ge(*arrived(item))
                if u >= 4:
                    act.wait_ge(*C.at("mm", u - 4))
                fn(wh[:, u % 4, :], raw_of(item)[:, j * HALF:(j + 1) * HALF], ACT.Copy).then_inc(*C.up("hi", u))

            def ada_rows(l, kind):
                act.wait_ge(*C.at("ada_mm", l, kind, DT - 1))
                step = next(b for b, items in PLAN.items() if (l, kind, DT - 1) in items)
                if step > LN_VAR[0]:
                    act.wait_ge(*C.at("ln_n", 0, CT - 1))
                else:
                    rotated = max(s for s in ROPE_AT[0] if s <= step)
                    act.wait_ge(*C.at("rope", 0, *BLOCKS[0][ROPE_AT[0][rotated]]))
                fn(adasb[:, :], psA[:, :], ACT.Copy).then_inc(*C.up("ada_rows", l, kind))

            def ada0_rows(quarter):
                act.wait_ge(*C.at("ada0_mm", SHIFT, quarter, 3))
                fn(T[:, 6, :], psA[:, :], ACT.Copy).then_inc(*C.up("ada0_rows", quarter))

            def square(l, m):
                n = TOK if l < LAYERS else LAT
                if l == 0:
                    act.wait_ge(*C.at(f"x_in{m // 4}"))
                else:
                    act.wait_ge(*C.at("evac_dve", (l - 1) * NB + B_OUT + m))
                if m >= 3:
                    act.wait_ge(*C.at("rms_add", l, m - 2))
                elif l:
                    act.wait_ge(*C.at("att_out", l - 1, max(groups(l - 1))))
                dst = T[:, 4 if m == 0 else 2 + m % 2, 0:n]
                fn(dst, Y[:, m, 0:n], ACT.Square).then_inc(*C.up("rms_sq", l, m))
                if l == LAYERS:
                    fn(Y[:, m, LAT:TOK], Y[:, m, 0:LAT], ACT.Copy, scale=at["final_g"][:, m:m + 1]).then_inc(*C.up("scaled", m))

            def rms_std(l):
                n = TOK if l < LAYERS else LAT
                act.wait_ge(*C.at("rms_mm", l))
                fn(tbuf[:, 0:n], psS[:, 0, 0:n], ACT.Sqrt, scale=1.0 / D, bias=eps[:, 0:1]).then_inc(*C.up("rms_std", l))

            def modulate(l, k):
                act.wait_ge(*C.at("mod", l, k, 1))
                for i in range(2):
                    fn(hh[:, k, i * LAT:(i + 1) * LAT], T[:, k % 2, i * LAT:(i + 1) * LAT], ACT.Identity,
                       bias=ada[:, l, i, SHIFT * DT + k:SHIFT * DT + k + 1]).then_inc(*C.up("h_hi", l, k, i))

            def evac(gb):
                l, b = divmod(gb, NB)
                kind, i = BLOCKS[l][b]
                n = width(l, b)
                if kind == "out":
                    return
                ps = bank(gb)[:, 0:n]
                act.wait_ge(*block_done(gb))
                if kind == "x":
                    act.wait_ge(*C.at("lrux_zero", l))
                    fn(lrux[:, i, :, LTAPS - 1:LTAPS - 1 + LAT], segs(ps), ACT.Copy).then_inc(*C.up("evac_act", gb))
                elif kind == "k":
                    fn(kT[:, i, :], ps, ACT.Copy).then_inc(*C.up("evac_act", gb))
                elif kind == "v":
                    if i:
                        act.wait_ge(*C.at("v_tp", l, i - 1))
                    elif l:
                        act.wait_ge(*C.at("evac_dve", l * NB + BLOCKS[l].index(("a", CT - 1))))
                    fn(tbuf[:, :], ps, ACT.Copy).then_inc(*C.up("evac_act", gb))
                elif kind == "b":
                    if i == 0:
                        act.wait_ge(*(C.at("h_lo", l, DT - 1) if l else C.at("v_tp", l, KV_HEADS - 1)))
                    else:
                        act.wait_ge(*C.at("evac_dve", gb - 1))
                    fn(tbuf[:, 0:n], ps, ACT.Tanh, scale=0.5).then_inc(*C.up("evac_act", gb))
                elif kind == "q":
                    if i == 0:
                        act.wait_ge(*C.at("lru_h", l, CT - 1))
                    fn(q[:, i, 0:n], ps, ACT.Copy).then_inc(*C.up("evac_act", gb))
                elif kind == "ag":
                    fn(Yv(l, 8 + i), ps, ACT.Tanh, scale=0.5).then_inc(*C.up("gate_tanh", gb))
                elif kind in ("lg", "cg"):
                    if (kind, i) != ("lg", 0):
                        act.wait_ge(*C.at("evac_dve", gb - 1))
                    fn(tbuf[:, 0:n], ps, ACT.Tanh, scale=0.5).then_inc(*C.up("gate_tanh", gb))

            def lru_act(l, t):
                act.wait_ge(*C.at("lru_mm", l, t))
                for d in range(2):
                    c = (l * 2 + d) * CT + t
                    fn(T[:, 4 * d + 1, :], psS[:, 2 * d, :], ACT.Tanh, scale=0.5, bias=hbr[:, c:c + 1]
                       ).then_inc(*C.up("lru_tanh", l, t, d, "r"))
                    fn(T[:, 4 * d + 2, :], psS[:, 2 * d + 1, :], ACT.Tanh, scale=0.5, bias=hbi[:, c:c + 1]
                       ).then_inc(*C.up("lru_tanh", l, t, d))
                for d in range(2):
                    c = (l * 2 + d) * CT + t
                    act.wait_ge(*C.ago("lru_tanh", 2 - 2 * d + 1))
                    fn(T[:, 4 * d + 3, :], T[:, 4 * d + 1, :], ACT.Exp, scale=s4n[:, c:c + 1], bias=s4n[:, c:c + 1]
                       ).then_inc(*C.up("lru_a", l, t, d))
                for d in range(2):
                    c = (l * 2 + d) * CT + t
                    act.wait_ge(*C.ago("lru_a", 1 - d))
                    fn(T[:, 4 * d + 1, :], T[:, 4 * d + 1, :], ACT.Tanh, scale=s4[:, c:c + 1], bias=s4[:, c:c + 1]
                       ).then_inc(*C.up("lru_t", l, t, d))
                for d in range(2):
                    fn(q[:, d, :], T[:, 4 * d + 3, :], ACT.Square).then_inc(*C.up("lru_a2", l, t, d))

            def lru_sqrt(l, t):
                for d in range(2):
                    act.wait_ge(*C.at("lru_v", l, t, d))
                    fn(q[:, d, :], q[:, d, :], ACT.Sqrt, scale=0.25).then_inc(*C.up("lru_sq", l, t, d))

            def att_exp(l, s):
                kv, qb, isctx = groups(l)[s]
                k0 = LAT if isctx else 0
                act.wait_ge(*C.at("att_neg", l, s))
                if s != min(groups(l)):
                    act.wait_ge(*C.at("p_tp", l, max(x for x in groups(l) if x < s), GROUP - 1))
                for g in range(GROUP):
                    fn(T[:, g, k0:TOK], psS[:, g, k0:TOK], ACT.Exp, scale=SCALE, bias=st[:, 1, g:g + 1],
                       accum_out=st[:, 2, g:g + 1]).then_inc(*C.up("att_exp", l, s, g))
                act.wait_ge(*C.at("att_sn", l, s))
                fn(st[:, 4, :], st[:, 3, :], ACT.Exp).then_inc(*C.up("att_es", l, s))
                act.wait_ge(*C.at("att_rden", l, s))
                for g in range(GROUP):
                    fn(T[:, g, k0:TOK], T[:, g, k0:TOK], ACT.Copy, scale=st[:, 5, g:g + 1]).then_inc(*C.up("probs", l, s, g))

            def att_pT(l, s):
                isctx = groups(l)[s][2]
                k0 = 2 if isctx else 0
                if s != min(groups(l)):
                    act.wait_ge(*C.at("pv", l, max(x for x in groups(l) if x < s)))
                for g in range(GROUP):
                    act.wait_ge(*C.at("p_tp", l, s, g))
                    fn(T[:, 4 + k0:8, g * QB:(g + 1) * QB],
                       psS[:, g, k0 * P:TOK].rearrange("p (k q) -> p k q", q=P), ACT.Copy).then_inc(*C.up("pT", l, s, g))

            def y_hi(l, b):
                for k in y_at(l, b):
                    if l == 0:
                        act.wait_ge(*C.at("mm", unit(l, B_OUT - 1, 0 if k < DT // 2 and b < B_OUT else 1)))
                    if k < CT:
                        act.wait_ge(*C.at("evac_dve", l * NB + B_OUT - CT + k))
                    else:
                        act.wait_ge(*C.at("evac_dve", l * NB + B_OUT - CT - 1))
                        act.wait_ge(*C.at("att_out", l, max(groups(l))))
                        act.wait_ge(*C.at("mm", 2 * (l * NB + B_Q) - 1))
                    fn(hh[:, k, y_parts(l)], Yv(l, k), ACT.Copy).then_inc(*C.up("y_hi", l, k))

            act.wait_ge(*C.at("small_in"))
            fn(tiny[:, 0, :], at["c"], ACT.Tanh, scale=0.5).then_inc(*C.up("c_tanh"))
            n = LAYERS * 2 * CT
            fn(tiny[:, 1, 0:n], at["lam"], ACT.Abs).then_inc(*C.up("lam_abs"))
            act.wait_ge(*C.ago("lam_abs"))
            fn(tiny[:, 1, 0:n], tiny[:, 1, 0:n], ACT.Exp, scale=-1.0).then_inc(*C.up("lam_exp"))
            act.wait_ge(*C.at("lam_one"))
            fn(tiny[:, 2, 0:n], tiny[:, 1, 0:n], ACT.Ln).then_inc(*C.up("lam_ln"))
            act.wait_ge(*C.at("exact_in"))
            fn(rounded[:, :, :], T[:, 5, 0:3 * P].rearrange("p (m k) -> p m k", m=3), ACT.Copy).then_inc(*C.up("rounded"))
            act.wait_ge(*C.at("eps_set"))
            for k in range(DT):
                square(0, k)
            for gb in range(GLOB):
                l, b = divmod(gb, NB)
                if b == 0:
                    if l:
                        square(l, DT - 1)
                        hi(2 * (gb - 1) + 5)
                    u0, n = unit(l, 0, 0), SIDE[l] // 2
                    if l == 0:
                        for quarter in range(4):
                            ada0_rows(quarter)
                            if quarter == 0:
                                rms_std(l)
                            u = open_unit(l, quarter, 0)
                            hi(u)
                            hi(u + 1)
                            for k in range(quarter * QT, (quarter + 1) * QT):
                                modulate(l, k)
                                if k % QT == 1:
                                    hi(u + 2)
                            if quarter > 1:
                                hi(u + 3)
                    else:
                        rms_std(l)
                        for quarter in range(4):
                            for k in range(quarter * QT, (quarter + 1) * QT):
                                modulate(l, k)
                            for i in range(n if 0 < quarter < 3 else 0):
                                hi(u0 + 4 + n * (quarter - 1) + i)
                    for i in range(4):
                        hi(u0 + 2 * OPEN[l] + i)
                        if i == 1 and l:
                            ada_rows(*PLAN[NB][-1][:2])
                        if i:
                            for c in range(2):
                                if 2 * (i - 1) + c < SIDE[l]:
                                    evac(gb + 2 * (i - 1) + c)
                    for c in range(SIDE[l], OPEN[l]):
                        evac(gb + c)
                if b < OPEN[l]:
                    continue
                if b == B_OUT:
                    y_hi(l, b)
                if gb + 2 < GLOB:
                    hi(2 * gb + 4)
                    if l == 0 and b == B_OUT - 1:
                        y_hi(l, b)
                    if b < NB - 1:
                        hi(2 * gb + 5)
                evac(gb)
                if b and BLOCKS[l][b - 1][0] == "v":
                    i = BLOCKS[l][b - 1][1]
                    act.wait_ge(*C.at("v_tp", l, i))
                    fn(v[:, :, i * HD:(i + 1) * HD], psM[:, :].rearrange("p (k d) -> p k d", d=HD), ACT.Copy
                       ).then_inc(*C.up("v_out", l, i))
                if b in LRU_SCAN[l]:
                    lru_sqrt(l, LRU_SCAN[l].index(b))
                if b in LRU_MM[l]:
                    lru_act(l, LRU_MM[l].index(b))
                if b - TP_LAG[l] in groups(l):
                    att_pT(l, b - TP_LAG[l])
                if l == 0:
                    for a in PLAN[b]:
                        if a[2] == DT - 1:
                            ada_rows(*a[:2])
                if b in groups(l):
                    att_exp(l, b)
                if b == LN_SUM[l]:
                    for t in range(CT):
                        act.wait_ge(*C.at("ln_c", l, t))
                        fn(glu_in(l, t), segs(Yv(l, t)), ACT.Square).then_inc(*C.up("ln_sq", l, t))
                if b == LN_VAR[l]:
                    n = width(l, b)
                    act.wait_ge(*C.at("ln_var", l))
                    fn(lnr[:, 0:n], psM[:, 0:n], ACT.Sqrt, scale=1.0 / (CT * P), bias=eps[:, 0:1]
                       ).then_inc(*C.up("ln_std", l))
                if b == LN_ACT[l]:
                    for t in range(CT):
                        c = l * CT + t
                        act.wait_ge(*C.at("ln_n", l, t))
                        fn(glu_in(l, t), segs(Yv(l, t)), ACT.Tanh, scale=lnhg[:, c:c + 1], bias=lnhb[:, c:c + 1]
                           ).then_inc(*C.up("ln_th", l, t))
                        fn(Yv(l, t), Yv(l, t), ACT.Identity, scale=at["ln_g"][:, c:c + 1], bias=at["ln_b"][:, c:c + 1]
                           ).then_inc(*C.up("ln_z", l, t))
                for m in range(CT if b == PW_AT else 0):
                    n = width(l, b)
                    c = l * CT + m
                    act.wait_ge(*C.at("pw_mm", l, m))
                    if m == 0:
                        act.wait_ge(*C.at("ln_y", l, CT - 1))
                    fn(glu_in(l, m), segs(pw_bank(l, m)[:, 0:n]), ACT.Identity, scale=0.5, bias=at["pw_b"][:, c:c + 1]
                       ).then_inc(*C.up("pw_out", l, m))
                if b - B_OUT >= 1:
                    square(l + 1, b - B_OUT - 1)
                if l and b != B_OUT:
                    y_hi(l, b)
            square(LAYERS, DT - 1)
            rms_std(LAYERS)

        @block.vector
        def _(dve):
            V = nc.vector
            stt = V.scalar_tensor_tensor

            def y_lo(l, b):
                for k in y_at(l, b):
                    dve.wait_ge(*C.at("y_hi", l, k))
                    V.tensor_tensor(hl[:, k, y_parts(l)], Yv(l, k), hh[:, k, y_parts(l)].bitcast(F32), ALU.subtract
                                    ).then_inc(*C.up("y_lo", l, k))

            def lo(u):
                item, j = source(u)
                dve.wait_ge(*C.at("hi", u))
                V.tensor_tensor(wl[:, u % 4, :], raw_of(item)[:, j * HALF:(j + 1) * HALF], wh[:, u % 4, :].bitcast(F32),
                                ALU.subtract).then_inc(*C.up("lo", u))

            def ada0_out(quarter):
                dve.wait_ge(*C.at("ada0_tp", quarter))
                ps = psA[:, :].rearrange("p (q j r) -> p r q j", q=4, j=4)
                for kind, rows in ((SCL, slice(0, 2)), (SHIFT, slice(2, 4))):
                    V.tensor_reduce(tiny[:, 1 + kind, 0:8].rearrange("p (r q) -> p r q", r=2), ps[:, rows], axis=AX.X,
                                    op=ALU.add).then_inc(*C.up("ada0_sum", kind, quarter))
                dve.wait_ge(*C.ago("ada0_sum"))
                for kind in (SCL, SHIFT):
                    at = kind * DT + quarter * QT
                    for i in range(2):
                        V.tensor_tensor(ada[:, 0, i, at:at + QT], tiny[:, 1 + kind, 4 * i:4 * i + 4], b_ada[:, 0, at:at + QT],
                                        ALU.add).then_inc(*C.up("ada_out", 0, kind, quarter))
                q4 = slice(quarter * QT, (quarter + 1) * QT)
                dve.wait_ge(*C.ago("ada_out"))
                for i in range(2):
                    stt(A[:, 0, i, q4], ada[:, 0, i, SCL * DT + quarter * QT:SCL * DT + (quarter + 1) * QT], 1.0,
                        norm_g[:, 0, q4], ALU.add, ALU.mult).then_inc(*C.up("A", 0, i))
                dve.wait_ge(*C.ago("A"))

            def rms_add(l, m):
                n = TOK if l < LAYERS else LAT
                dve.wait_ge(*C.at("rms_sq", l, m))
                if m == 0:
                    return
                if m > 1:
                    dve.wait_ge(*C.ago("rms_add"))
                V.tensor_tensor(T[:, 4, 0:n], T[:, 4, 0:n], T[:, 2 + m % 2, 0:n], ALU.add
                                ).then_inc(*(C.up("rms_add", l, m)))

            def ada_out(l, kind):
                dve.wait_ge(*C.at("ada_tp", l, kind))
                cols = psA[:, :].rearrange("p (q j r) -> p q j r", q=4, j=4)
                for i in range(2):
                    V.tensor_tensor(ada[:, l, i, kind * DT:(kind + 1) * DT].rearrange("p (j q) -> p q j", q=4),
                                    cols[:, :, :, i], b_ada[:, l, kind * DT:(kind + 1) * DT].rearrange("p (j q) -> p q j", q=4),
                                    ALU.add).then_inc(*C.up("ada_out", l, kind))
                if kind == SCL:
                    for i in range(2):
                        dve.wait_ge(*C.ago("ada_out", 0))
                        stt(A[:, l, i, :], ada[:, l, i, SCL * DT:(SCL + 1) * DT], 1.0, norm_g[:, l, :], ALU.add, ALU.mult
                            ).then_inc(*C.up("A", l, i))

            def modulate(l, k):
                for i in range(2):
                    w = slice(i * LAT, (i + 1) * LAT)
                    stt(T[:, k % 2, w], Y[:, k, w], A[:, l, i, k:k + 1], tbuf[:, w], ALU.mult, ALU.mult
                        ).then_inc(*C.up("mod", l, k, i))

            def h_lo(l, k):
                for i in range(2):
                    w = slice(i * LAT, (i + 1) * LAT)
                    dve.wait_ge(*C.at("h_hi", l, k, i))
                    stt(hl[:, k, w], T[:, k % 2, w], ada[:, l, i, SHIFT * DT + k:SHIFT * DT + k + 1],
                        hh[:, k, w].bitcast(F32), ALU.add, ALU.subtract).then_inc(*C.up("h_lo", l, k))

            def rstd(l):
                n = TOK if l < LAYERS else LAT
                dve.wait_ge(*C.at("rms_std", l))
                V.reciprocal(tbuf[:, 0:n], tbuf[:, 0:n]).then_inc(*C.up("rstd", l))
                dve.wait_ge(*C.ago("rstd"))

            def h_quarter(l, quarter, u=None):
                for k in range(quarter * QT, (quarter + 1) * QT):
                    if l and k < 2:
                        dve.wait_ge(*C.ago("evac_dve"))
                    if k >= 2:
                        dve.wait_ge(*C.at("h_lo", l, k - 2))
                    modulate(l, k)
                    if k > quarter * QT:
                        h_lo(l, k - 1)
                    if k % QT == 2 and u is not None:
                        lo(u)
                h_lo(l, (quarter + 1) * QT - 1)

            def evac(gb):
                l, b = divmod(gb, NB)
                kind, i = BLOCKS[l][b]
                n = width(l, b)
                ps = bank(gb)[:, 0:n]
                if kind == "a":
                    dve.wait_ge(*C.at("mm", 2 * gb + 1))
                    dve.wait_ge(*C.at("evac_act", gb - 1))
                    dve.wait_ge(*C.at("glu_zero"))
                    stt(glu_in(l, i), segs(tbuf[:, 0:n]), 1.0, segs(ps), ALU.add, ALU.mult).then_inc(*C.up("evac_dve", gb))
                elif kind == "ag":
                    dve.wait_ge(*C.at("gate_tanh", gb))
                    stt(Yv(l, 8 + i), Yv(l, 8 + i), 1.0, ps, ALU.add, ALU.mult).then_inc(*C.up("evac_dve", gb))
                elif kind in ("lg", "cg"):
                    dve.wait_ge(*C.at("gate_tanh", gb))
                    stt(tbuf[:, 0:n], tbuf[:, 0:n], 1.0, ps, ALU.add, ALU.mult).then_inc(*C.up("gated", gb))
                    dve.wait_ge(*C.ago("gated"))
                    if kind == "lg":
                        stt(Yv(l, 4 + i), tbuf[:, 0:n], 0.5, Yv(l, 4 + i), ALU.mult, ALU.mult
                            ).then_inc(*C.up("evac_dve", gb))
                    else:
                        dve.wait_ge(*C.at("pw_out", l, i))
                        if i == 0:
                            dve.wait_ge(*C.at("pw_mm", l, CT - 1))
                        stt(segs(Yv(l, i)), segs(tbuf[:, 0:n]), 0.5, glu_in(l, i), ALU.mult, ALU.mult
                            ).then_inc(*C.up("evac_dve", gb))
                elif kind == "out":
                    dve.wait_ge(*C.at("mm", 2 * gb + 1))
                    if l == 0:
                        dve.wait_ge(*C.at(f"xs{i % 2}", i))
                    for s in range(n // LAT):
                        w = slice(s * LAT, (s + 1) * LAT)
                        old = T[:, i % 2, w] if l == 0 else Y[:, i, w]
                        stt(Y[:, i, w], ps[:, w], ada[:, l, s, GATE * DT + i:GATE * DT + i + 1], old, ALU.mult, ALU.add
                            ).then_inc(*C.up("evac_dve", gb))

            def rope(l, b):
                kind, i = BLOCKS[l][b]
                x = kT[:, i, 0:LAT] if kind == "k" else q[:, i, 0:LAT]
                dve.wait_ge(*C.at("rope_mm", l, kind, i))
                if (l, kind, i) != (0, "k", 0):
                    dve.wait_ge(*C.ago("rope"))
                V.tensor_tensor(lnr[:, 0:LAT], psM[:, 0:LAT], sin, ALU.mult).then_inc(*C.up("rope_t", l, kind, i))
                V.tensor_tensor(x, x, cos, ALU.mult).then_inc(*C.up("rope_c", l, kind, i))
                dve.wait_ge(*C.ago("rope_c"))
                V.tensor_tensor(x, x, lnr[:, 0:LAT], ALU.add).then_inc(*C.up("rope", l, kind, i))

            def taps(l, t):
                if t == 0:
                    dve.wait_ge(*C.ago("h_lo"))
                dve.wait_ge(*C.at("evac_act", l * NB + t))
                if t:
                    dve.wait_ge(*C.ago("lru_h"))
                for k in range(LTAPS):
                    for d in range(2):
                        c = (l * 2 + d) * CT + t
                        s = k if d == 0 else 2 * (LTAPS - 1) - k
                        x = lrux[:, t, :, s:s + LAT]
                        out = segs(T[:, 4 * d, :])
                        if k == 0:
                            V.tensor_scalar(out, x, lcw[:, c, 0:1], at["lcb"][:, c:c + 1], ALU.mult, ALU.add
                                            ).then_inc(*C.up("taps", l, t, d))
                        else:
                            dve.wait_ge(*C.ago("taps", 1))
                            stt(out, x, lcw[:, c, k:k + 1], out, ALU.mult, ALU.add).then_inc(*C.up("taps", l, t, d))

            def lru_v(l, t):
                for d in range(2):
                    dve.wait_ge(*C.at("lru_a2", l, t, d))
                    stt(q[:, d, :], q[:, d, :], 1.0, T[:, 4 * d + 1, :], ALU.add, ALU.mult).then_inc(*C.up("lru_v", l, t, d))
                for d in range(2):
                    stt(T[:, 4 * d + 2, :], T[:, 4 * d + 2, :], 1.0, T[:, 4 * d, :], ALU.add, ALU.mult
                        ).then_inc(*C.up("lru_g", l, t, d))

            def lru_scan(l, t):
                for d in range(2):
                    dve.wait_ge(*C.at("lru_sq", l, t, d))
                    dve.wait_ge(*C.ago("lru_g"))
                    V.tensor_tensor(T[:, 4 * d + 2, :], T[:, 4 * d + 2, :], q[:, d, :], ALU.mult
                                    ).then_inc(*C.up("lru_b", l, t, d))
                dve.wait_ge(*C.ago("lru_b", 1))
                f, r = T[:, 0, :], T[:, 4, :]
                V.tensor_tensor_scan(f[:, LAT:TOK], T[:, 3, LAT:TOK], T[:, 2, LAT:TOK], 0.0, ALU.mult, ALU.add
                                     ).then_inc(*C.up("lru_scan", l, t))
                dve.wait_ge(*C.ago("lru_b"))
                V.tensor_tensor_scan(r[:, ::-1], T[:, 7, ::-1], T[:, 6, ::-1], 0.0, ALU.mult, ALU.add
                                     ).then_inc(*C.up("lru_scan", l, t))
                dve.wait_ge(*C.ago("lru_scan", 1))
                V.tensor_tensor_scan(f[:, 0:LAT], T[:, 3, 0:LAT], T[:, 2, 0:LAT], f[:, TOK - 1:TOK], ALU.mult, ALU.add
                                     ).then_inc(*C.up("lru_scan", l, t))
                dve.wait_ge(*C.ago("lru_scan"))
                n = TOK if l == 0 else LAT
                V.tensor_tensor(Yv(l, 4 + t), f[:, 0:n], r[:, 0:n], ALU.add).then_inc(*C.up("lru_h", l, t))

            def conv(l, pairs):
                for t, k in pairs:
                    c = (l * CT + t) * TAPS + k
                    x = glu[:, t, 0:(2 if l == 0 else 1), k:k + LAT]
                    out = segs(Yv(l, t))
                    if k == 0:
                        dve.wait_ge(*C.ago("evac_dve"))
                        V.tensor_scalar(out, x, dwh[:, c:c + 1], at["dw_b"][:, l * CT + t:l * CT + t + 1], ALU.mult,
                                        ALU.add).then_inc(*C.up("conv", l, t, k))
                    else:
                        dve.wait_ge(*C.ago("conv", 1))
                        stt(out, x, dwh[:, c:c + 1], out, ALU.mult, ALU.add).then_inc(*C.up("conv", l, t, k))

            def ln_add(l, stage):
                acc = lnr[:, 0:TOK if l == 0 else LAT]
                if stage == "ln_var":
                    acc = acc if l else segs(acc)
                for t in range(1, CT):
                    if stage == "ln_sum":
                        x, y = Yv(l, t), Yv(l, 0)
                        dve.wait_ge(*C.ago("conv" if t == 1 else "ln_add"))
                    else:
                        x, y = (glu_in(l, t), glu_in(l, 0)) if l == 0 else (glu[:, t, 0, PAD:PAD + LAT], glu[:, 0, 0, PAD:PAD + LAT])
                        dve.wait_ge(*C.at("ln_sq", l, t))
                        if t > 1:
                            dve.wait_ge(*C.ago("ln_add"))
                    V.tensor_tensor(acc, y if t == 1 else acc, x, ALU.add).then_inc(*C.up("ln_add", l, stage))

            def att_max(l, s):
                kv, qb, isctx = groups(l)[s]
                k0 = LAT if isctx else 0
                h = l * HEADS + GROUP * kv
                dve.wait_ge(*C.at("scores", l, s))
                V.tensor_reduce(st[:, 0, :], psS[:, :, k0:TOK], axis=AX.X, op=ALU.max).then_inc(*C.up("att_max", l, s))
                dve.wait_ge(*C.ago("att_max"))
                stt(st[:, 1, :], st[:, 0, :], -SCALE, nsink[:, h:h + GROUP], ALU.mult, ALU.min).then_inc(*C.up("att_neg", l, s))
                dve.wait_ge(*C.ago("att_neg"))
                V.tensor_tensor(st[:, 3, :], st[:, 1, :], sink[:, h:h + GROUP], ALU.add).then_inc(*C.up("att_sn", l, s))

            def att_norm(l, s):
                isctx = groups(l)[s][2]
                k0 = LAT if isctx else 0
                dve.wait_ge(*C.at("att_es", l, s))
                V.tensor_tensor(st[:, 5, :], st[:, 2, :], st[:, 4, :], ALU.add).then_inc(*C.up("att_den", l, s))
                dve.wait_ge(*C.ago("att_den"))
                V.reciprocal(st[:, 5, :], st[:, 5, :]).then_inc(*C.up("att_rden", l, s))

            def att_out(l, s):
                kv, qb, isctx = groups(l)[s]
                t0 = (LAT if isctx else 0) + qb * QB
                y = (Y if l == 0 else Y[:, :, LAT:TOK])[:, 8 + GROUP * kv:8 + GROUP * kv + GROUP, t0:t0 + QB]
                dve.wait_ge(*C.at("pv", l, s))
                stt(y, psS[:, 0, :].rearrange("p (g t) -> p g t", g=GROUP), 0.5, y, ALU.mult, ALU.mult
                    ).then_inc(*C.up("att_out", l, s))

            dve.wait_ge(*C.at("c_tanh"))
            stt(tiny[:, 0, :], tiny[:, 0, :], 1.0, at["c"], ALU.add, ALU.mult).then_inc(*C.up("cstat", 0))
            dve.wait_ge(*C.at("cstat_zero"))
            dve.wait_ge(*C.ago("cstat"))
            V.tensor_scalar(cstat[:, :, 2:4], tiny[:, 0, :].rearrange("p (k v) -> p k v", v=2), 0.5, None, ALU.mult
                            ).then_inc(*C.up("cstat", 1))
            n = LAYERS * 2 * CT
            dve.wait_ge(*C.at("lam_exp"))
            V.tensor_scalar(tiny[:, 1, 0:n], tiny[:, 1, 0:n], 1.0, None, ALU.add).then_inc(*C.up("lam_one"))
            V.tensor_scalar(tiny[:, 1, 16:16 + n], at["lam"], -1.0, 0.0, ALU.mult, ALU.max).then_inc(*C.up("derived"))
            dve.wait_ge(*C.at("lam_ln"))
            dve.wait_ge(*C.ago("derived"))
            V.tensor_tensor(tiny[:, 2, 0:n], tiny[:, 2, 0:n], tiny[:, 1, 16:16 + n], ALU.add).then_inc(*C.up("derived"))
            dve.wait_ge(*C.ago("derived"))
            for dst, src, f in ((s4, tiny[:, 2, 0:n], 4.0), (s4n, tiny[:, 2, 0:n], -4.0), (dwh, at["dw_w"], 0.5),
                                (hbr, at["b_r"], 0.5), (hbi, at["b_i"], 0.5), (lnhg, at["ln_g"], 0.5),
                                (lnhb, at["ln_b"], 0.5), (nsink, sink, -1.0)):
                V.tensor_scalar(dst, src, f, None, ALU.mult).then_inc(*C.up("derived"))
            dve.wait_ge(*C.ago("derived"))

            for m in range(DT - 1):
                rms_add(0, m)
            for gb in range(GLOB):
                l, b = divmod(gb, NB)
                if b == 0:
                    u0, n = unit(l, 0, 0), SIDE[l] // 2
                    if l == 0:
                        for quarter in range(4):
                            ada0_out(quarter)
                            if quarter == 0:
                                rstd(l)
                            u = open_unit(l, quarter, 0)
                            lo(u)
                            lo(u + 1)
                            h_quarter(l, quarter, u + 2)
                            if quarter > 1:
                                lo(u + 3)
                    else:
                        lo(2 * (gb - 1) + 5)
                        rstd(l)
                        for quarter in range(4):
                            h_quarter(l, quarter)
                            for i in range(n if 0 < quarter < 3 else 0):
                                lo(u0 + 4 + n * (quarter - 1) + i)
                    for i in range(4):
                        lo(u0 + 2 * OPEN[l] + i)
                if b < OPEN[l]:
                    continue
                if b == B_OUT:
                    y_lo(l, b)
                if gb + 2 < GLOB:
                    lo(2 * gb + 4)
                if l == 0 and b == B_OUT - 1:
                    y_lo(l, b)
                for a in done_before(l, b):
                    ada_out(*a)
                if b - TP_LAG[l] - 1 in groups(l):
                    att_out(l, b - TP_LAG[l] - 1)
                if gb + 2 < GLOB and b < NB - 1:
                    lo(2 * gb + 5)
                evac(gb)
                if b in ROPE_AT[l]:
                    rope(l, ROPE_AT[l][b])
                if b in groups(l):
                    att_max(l, b)
                if b in LRU_MM[l]:
                    lru_v(l, LRU_MM[l].index(b))
                if b in LRU_SCAN[l]:
                    lru_scan(l, LRU_SCAN[l].index(b))
                if b in LRU_TAPS[l]:
                    taps(l, LRU_TAPS[l].index(b))
                conv(l, conv_taps(l, b))
                if b in groups(l):
                    att_norm(l, b)
                if b == LN_SUM[l] - 1:
                    ln_add(l, "ln_sum")
                if b == LN_SUM[l]:
                    n = width(l, b)
                    dve.wait_ge(*C.at("ln_sum", l))
                    for t in range(CT):
                        stt(Yv(l, t), psM[:, 0:n], -1.0 / (CT * P), Yv(l, t), ALU.mult, ALU.add).then_inc(*C.up("ln_c", l, t))
                    ln_add(l, "ln_var")
                if b == LN_VAR[l]:
                    n = width(l, b)
                    dve.wait_ge(*C.at("ln_std", l))
                    V.reciprocal(lnr[:, 0:n], lnr[:, 0:n]).then_inc(*C.up("ln_rstd", l))
                    dve.wait_ge(*C.ago("ln_rstd"))
                    for t in range(CT):
                        V.tensor_tensor(Yv(l, t), Yv(l, t), lnr[:, 0:n], ALU.mult).then_inc(*C.up("ln_n", l, t))
                if b == LN_ACT[l]:
                    for t in range(CT):
                        dve.wait_ge(*C.at("ln_z", l, t))
                        stt(segs(Yv(l, t)), glu_in(l, t), 1.0, segs(Yv(l, t)), ALU.add, ALU.mult).then_inc(*C.up("ln_y", l, t))

                if l and b != B_OUT:
                    y_lo(l, b)
                if b > B_OUT:
                    rms_add(l + 1, b - B_OUT - 1)

            rstd(LAYERS)
            dve.wait_ge(*C.ago("evac_dve"))
            for m in range(0, DT, FINAL):
                for k in range(m, m + FINAL):
                    dve.wait_ge(*C.at("scaled", k))
                V.tensor_tensor(Y[:, m:m + FINAL, 0:LAT], Y[:, m:m + FINAL, LAT:TOK],
                                tbuf[:, 0:LAT].unsqueeze(1).to_broadcast([P, FINAL, LAT]), ALU.mult).then_inc(*C.up("final", m))
        return dict(C.marks)


def _tables():
    ident = np.eye(P, dtype=np.float32)
    perm = np.zeros((P, P), np.float32)
    for m in range(P):
        perm[m + 32 if m % 64 < 32 else m - 32, m] = -1.0 if m % 64 < 32 else 1.0
    half = HD // 2
    inv = np.float32(10000.0) ** (-np.arange(0, half, 2, dtype=np.float32) / np.float32(half))
    t = np.arange(LAT)
    row, col = (t // 64).astype(np.float32), (t % 64).astype(np.float32)
    ang = np.concatenate([row[:, None] * inv, row[:, None] * inv, col[:, None] * inv, col[:, None] * inv], axis=1).T
    a, b = np.arange(P)[None, :], np.arange(P)[:, None]
    mask = np.stack([np.where(a > b, MASKED, 0.0), np.where(a < b, MASKED, 0.0)], axis=1).astype(np.float32)
    return {"ident": ident, "ones": np.ones((P, P), np.float32), "perm": perm,
            "cos": np.cos(ang).astype(np.float32), "sin": np.sin(ang).astype(np.float32), "mask": mask}


def _lay_out(x, c, ctx, c_ctx, norm_g, w_ada, b_ada, w_in, dw_w, dw_b, ln_g, ln_b, pw_w, pw_b, lru_conv_w,
             lru_conv_b, lru_w_r, lru_b_r, lru_w_i, lru_b_i, lru_lam, attn_sink, w_out, final_g):
    def cols(a):
        a = a.reshape(*a.shape[:-1], -1, P)
        return np.moveaxis(a, -1, 0).reshape(P, -1)

    small = _tables()
    small.update(
        c=np.stack([c[0].reshape(DT, P).T, c_ctx.reshape(DT, P).T], axis=2), norm_g=cols(norm_g), final_g=cols(final_g),
        b_ada=cols(b_ada), dw_w=np.moveaxis(dw_w.reshape(LAYERS, TAPS, CT, P), (3, 0, 2, 1), (0, 1, 2, 3)),
        dw_b=cols(dw_b), ln_g=cols(ln_g), ln_b=cols(ln_b), pw_b=cols(pw_b),
        lcw=lru_conv_w.reshape(LAYERS, 2, LTAPS, CT, P).transpose(4, 0, 1, 3, 2), lcb=cols(lru_conv_b),
        b_r=cols(lru_b_r), b_i=cols(lru_b_i), lam=cols(lru_lam),
        sink=np.broadcast_to(attn_sink.reshape(1, -1), (P, LAYERS * HEADS)))
    exact = np.concatenate([small["ident"], small["mask"].reshape(P, 2 * P)], axis=1)
    packed = np.concatenate([np.ascontiguousarray(small[name]).reshape(P, n) for name, n in SMALL], axis=1)
    blocks = []
    for l in range(LAYERS):
        for kind, i in BLOCKS[l]:
            w, at = (w_out[l], i * P) if kind == "out" else (w_in[l], COLUMN[kind] + i * P)
            w = w[:, at:at + P].reshape(DT, P, P)
            if kind == "out":
                w = np.roll(w, -CT, axis=0)
            blocks.append(w.transpose(1, 0, 2).reshape(P, DT * P))
    lru = np.stack([lru_w_r, lru_w_i], axis=1)
    lru = lru.reshape(LAYERS, 2, 2, CT, 2, 64, 64).transpose(0, 1, 4, 5, 2, 3, 6).reshape(LAYERS, 2, 2, 64, 2 * CT, 64)
    tokens = np.concatenate([x[0], ctx[0]], axis=0)
    return {
        "small": packed, "exact": exact, "w_blocks": np.stack(blocks), "w_ada": w_ada,
        "pw": pw_w.reshape(LAYERS, CT, P, CT, P).transpose(0, 2, 3, 1, 4).reshape(LAYERS, P, CT * CT * P),
        "lru_w": lru, "xT": tokens.T.reshape(DT, P, TOK).transpose(1, 0, 2),
    }


def kernel(**inputs):
    import concourse.bacc as bacc
    from concourse.bass_utils import run_bass_kernel_spmd

    arrays = {n: np.ascontiguousarray(a) for n, a in _lay_out(**{n: np.asarray(a) for n, a in inputs.items()}).items()}

    def build(known):
        nc = bacc.Bacc("TRN2", target_bir_lowering=False, num_devices=1, dynamic_dma_scratch_size=64)
        io = {n: nc.dram_tensor("in_" + n, a.shape, mybir.dt.from_np(a.dtype), kind="ExternalInput").ap()
              for n, a in arrays.items()}
        io["out"] = nc.dram_tensor("out", (P, DT, LAT), F32, kind="ExternalOutput").ap()
        return nc, program(nc, io, known)

    marks = build({})[1]
    nc = build(marks)[0]
    r = run_bass_kernel_spmd(nc, [{"in_" + n: a for n, a in arrays.items()}], core_ids=[0])
    return r.results[0]["out"].transpose(1, 0, 2).reshape(D, LAT).T.reshape(1, LAT, D)
```
